# Optimizing a Trainium2 kernel written in Bass

```python
import jax, jax.numpy as jnp
from jax import lax
import numpy as np

D_MODEL = 1024
BATCH = 1
SEQ = 1024
DEPTH = 1
DEC_BATCH = 1
DEC_SEQ = 32
PAST_LEN = 512

CHUNK = 64
D_PLE = 256
D_MIX = D_MODEL
D_A = D_MIX // 4
H_A = 4
GMLP_CHUNK = 128
D_B = D_MIX // 4
CONV_W = 3
D_C = D_MIX // 2
H_C = 4
DV_C = D_C // H_C
DK_C = DV_C // 2
GATE_RANK = 16
GATE_TAU = 16.0
D_FF = 2816
EPS = 1e-6

SPLIT_SIZES = (D_A, D_A, D_B, D_B, D_B, H_C * DK_C, H_C * DK_C, D_C, D_C, GATE_RANK)
P_TOT = sum(SPLIT_SIZES)
SPLIT_IDX = tuple(int(s) for s in np.cumsum(SPLIT_SIZES)[:-1])

kernel_name = "hybrid_streaming_gmlp_conv_gla_step"

def rms_norm(x, g):
    xf = x.astype(jnp.float32)
    y = xf * lax.rsqrt(jnp.mean(xf * xf, axis=-1, keepdims=True) + EPS)
    return (y * g.astype(jnp.float32)).astype(x.dtype)

def swiglu(x, wg, wu, wd):
    return (jax.nn.silu(x @ wg) * (x @ wu)) @ wd

def block_causal_mask(L):
    i = np.arange(L)
    return ((i[None, :] // CHUNK) <= (i[:, None] // CHUNK)).astype(np.float32)

def gmlp_mix(u, v, w_s, b_s):
    bsz, t, _ = v.shape
    L = min(t, GMLP_CHUNK)
    vf = v.astype(jnp.float32)
    mu = jnp.mean(vf, axis=-1, keepdims=True)
    var = jnp.mean(jnp.square(vf - mu), axis=-1, keepdims=True)
    vn = (vf - mu) * lax.rsqrt(var + EPS)
    vh = vn.reshape(bsz, t // L, L, H_A, D_A // H_A)
    W = w_s[:, :L, :L].astype(jnp.float32) * block_causal_mask(L)
    bias = b_s[:, :L].astype(jnp.float32).T[None, None, :, :, None]
    s = jnp.einsum('hij,bnjhd->bnihd', W, vh) + bias
    y = (u.astype(jnp.float32) * s.reshape(bsz, t, D_A)).astype(u.dtype)
    return y, vn.astype(v.dtype)

def short_conv(b, c, xin, hist, conv_w):
    z = c * xin
    t = z.shape[1]
    zp = jnp.concatenate([hist.astype(z.dtype), z], axis=1)
    y = sum(conv_w[j] * zp[:, j:j + t] for j in range(CONV_W))
    return b * y, zp[:, -(CONV_W - 1):]

def gla_recurrence(q, k, v, g, s0, L):
    bsz, t, h, _ = q.shape
    n = t // L
    f32 = jnp.float32
    q = q.astype(f32).reshape(bsz, n, L, h, DK_C) * (DK_C ** -0.5)
    k = k.astype(f32).reshape(bsz, n, L, h, DK_C)
    v = v.astype(f32).reshape(bsz, n, L, h, DV_C)
    G = jnp.cumsum(g.astype(f32).reshape(bsz, n, L, h, DK_C), axis=2)
    G_last = G[:, :, -1:]
    q_t = q * jnp.exp(G)
    k_t = k * jnp.exp(-G)
    k_e = k * jnp.exp(G_last - G)
    A = jnp.einsum('bnihk,bnjhk->bnhij', q_t, k_t)
    A = jnp.where(np.tril(np.ones((L, L), dtype=bool)), A, 0.0)
    o_intra = jnp.einsum('bnhij,bnjhv->bnihv', A, v)
    dS = jnp.einsum('bnjhk,bnjhv->nbhkv', k_e, v)
    decay = jnp.exp(G_last[:, :, 0]).transpose(1, 0, 2, 3)

    def step(S, inp):
        a, d = inp
        return a[..., None] * S + d, S

    s_fin, s_prev = lax.scan(step, s0.astype(f32), (decay, dS))
    o_inter = jnp.einsum('bnihk,nbhkv->bnihv', q_t, s_prev)
    o = (o_intra + o_inter).reshape(bsz, t, h, DV_C)
    return o, s_fin

def gla_mixer(q, k, v, r, g_low, w_gate2, b_gate2, gla_norm, s0):
    bsz, t, _ = q.shape
    g = jax.nn.log_sigmoid((g_low @ w_gate2 + b_gate2).astype(jnp.float32)) / GATE_TAU
    o, s_fin = gla_recurrence(q.reshape(bsz, t, H_C, DK_C), k.reshape(bsz, t, H_C, DK_C),
                              v.reshape(bsz, t, H_C, DV_C), g.reshape(bsz, t, H_C, DK_C),
                              s0, min(t, CHUNK))
    o = o * lax.rsqrt(jnp.mean(o * o, axis=-1, keepdims=True) + EPS)
    o = o * gla_norm.astype(jnp.float32).reshape(H_C, DV_C)
    y = o.reshape(bsz, t, D_C).astype(r.dtype) * jax.nn.silu(r)
    return y, s_fin

def trunk_layer(x, p, conv_hist, gla_s0, lw):
    (n_f1, wg1, wu1, wd1, n_mix, w_in, w_s, b_s, conv_w, w_gate2, b_gate2, gla_norm, w_o,
     n_f2, wg2, wu2, wd2, n_ple, w_ple_gate, w_ple_proj) = lw
    x = x + 0.5 * swiglu(rms_norm(x, n_f1), wg1, wu1, wd1)
    h = rms_norm(x, n_mix) @ w_in
    u_a, v_a, b_b, c_b, x_b, q_c, k_c, v_c, r_c, g_low = jnp.split(h, SPLIT_IDX, axis=-1)
    y_a, v_rows = gmlp_mix(u_a, v_a, w_s, b_s)
    y_b, conv_new = short_conv(b_b, c_b, x_b, conv_hist, conv_w)
    y_c, s_new = gla_mixer(q_c, k_c, v_c, r_c, g_low, w_gate2, b_gate2, gla_norm, gla_s0)
    x = x + jnp.concatenate([y_a, y_b, y_c], axis=-1) @ w_o
    x = x + 0.5 * swiglu(rms_norm(x, n_f2), wg2, wu2, wd2)
    gate = jax.nn.sigmoid(rms_norm(x, n_ple) @ w_ple_gate)
    x = x + gate * (p.astype(x.dtype) @ w_ple_proj)
    return x, conv_new, s_new, v_rows

def setup_inputs(seed: int = 0) -> dict:
    key = jax.random.key(seed)
    ks = jax.random.split(key, 32)

    def nrm(k, shape, scale=1.0):
        return jax.random.normal(k, shape, jnp.float32) * scale

    def gain(k, shape):
        return 1.0 + 0.05 * jax.random.normal(k, shape, jnp.float32)

    return {
        "x_prompt": nrm(ks[0], (BATCH, SEQ, D_MODEL)),
        "x_sample": nrm(ks[1], (DEC_BATCH, DEC_SEQ, D_MODEL)),
        "p_prompt": nrm(ks[2], (DEPTH, BATCH, SEQ, D_PLE)),
        "p_sample": nrm(ks[3], (DEPTH, DEC_BATCH, DEC_SEQ, D_PLE)),
        "state_conv": nrm(ks[4], (DEPTH, DEC_BATCH, CONV_W - 1, D_B)),
        "state_gla": nrm(ks[5], (DEPTH, DEC_BATCH, H_C, DK_C, DV_C), 0.5),
        "norm_ffn1": gain(ks[6], (DEPTH, D_MODEL)),
        "w_ffn1_gate": nrm(ks[7], (DEPTH, D_MODEL, D_FF), D_MODEL ** -0.5),
        "w_ffn1_up": nrm(ks[8], (DEPTH, D_MODEL, D_FF), D_MODEL ** -0.5),
        "w_ffn1_down": nrm(ks[9], (DEPTH, D_FF, D_MODEL), D_FF ** -0.5),
        "norm_mix": gain(ks[10], (DEPTH, D_MODEL)),
        "w_in": nrm(ks[11], (DEPTH, D_MODEL, P_TOT), D_MODEL ** -0.5),
        "w_s": nrm(ks[12], (DEPTH, H_A, GMLP_CHUNK, GMLP_CHUNK), GMLP_CHUNK ** -0.5),
        "b_s": 1.0 + 0.01 * jax.random.normal(ks[13], (DEPTH, H_A, GMLP_CHUNK), jnp.float32),
        "conv_w": nrm(ks[14], (DEPTH, CONV_W, D_B), CONV_W ** -0.5),
        "w_gate2": nrm(ks[15], (DEPTH, GATE_RANK, H_C * DK_C), GATE_RANK ** -0.5),
        "b_gate2": nrm(ks[16], (DEPTH, H_C * DK_C), 0.1),
        "gla_norm": gain(ks[17], (DEPTH, D_C)),
        "w_o": nrm(ks[18], (DEPTH, D_MIX, D_MODEL), D_MIX ** -0.5),
        "norm_ffn2": gain(ks[19], (DEPTH, D_MODEL)),
        "w_ffn2_gate": nrm(ks[20], (DEPTH, D_MODEL, D_FF), D_MODEL ** -0.5),
        "w_ffn2_up": nrm(ks[21], (DEPTH, D_MODEL, D_FF), D_MODEL ** -0.5),
        "w_ffn2_down": nrm(ks[22], (DEPTH, D_FF, D_MODEL), D_FF ** -0.5),
        "norm_ple": gain(ks[23], (DEPTH, D_MODEL)),
        "w_ple_gate": nrm(ks[24], (DEPTH, D_MODEL, D_MODEL), D_MODEL ** -0.5),
        "w_ple_proj": nrm(ks[25], (DEPTH, D_PLE, D_MODEL), D_PLE ** -0.5),
        "final_norm": gain(ks[26], (D_MODEL,)),
    }

def reference(x_prompt, x_sample, p_prompt, p_sample, state_conv, state_gla,
              norm_ffn1, w_ffn1_gate, w_ffn1_up, w_ffn1_down, norm_mix, w_in, w_s, b_s,
              conv_w, w_gate2, b_gate2, gla_norm, w_o, norm_ffn2, w_ffn2_gate, w_ffn2_up,
              w_ffn2_down, norm_ple, w_ple_gate, w_ple_proj, final_norm):
    xp, xs = x_prompt, x_sample
    bp = x_prompt.shape[0]
    conv_hist_p = jnp.zeros((bp, CONV_W - 1, D_B), x_prompt.dtype)
    gla_s0_p = jnp.zeros((bp, H_C, DK_C, DV_C), jnp.float32)
    conv_p, gla_p, conv_s, gla_s, vrow_s = [], [], [], [], []
    for i in range(DEPTH):
        lw = (norm_ffn1[i], w_ffn1_gate[i], w_ffn1_up[i], w_ffn1_down[i], norm_mix[i], w_in[i],
              w_s[i], b_s[i], conv_w[i], w_gate2[i], b_gate2[i], gla_norm[i], w_o[i],
              norm_ffn2[i], w_ffn2_gate[i], w_ffn2_up[i], w_ffn2_down[i], norm_ple[i],
              w_ple_gate[i], w_ple_proj[i])
        xp, cp, sp, _ = trunk_layer(xp, p_prompt[i], conv_hist_p, gla_s0_p, lw)
        xs, cs, ss, vs = trunk_layer(xs, p_sample[i], state_conv[i], state_gla[i], lw)
        conv_p.append(cp)
        gla_p.append(sp)
        conv_s.append(cs)
        gla_s.append(ss)
        vrow_s.append(vs)
    y_prompt = rms_norm(xp, final_norm)
    y_sample = rms_norm(xs, final_norm)
    conv_prompt = jnp.stack(conv_p)
    gla_prompt = jnp.stack(gla_p)
    conv_sample = jnp.stack(conv_s)
    gla_sample = jnp.stack(gla_s)
    gmlp_v_sample = jnp.stack(vrow_s)
    return (y_prompt, y_sample, conv_prompt, gla_prompt, conv_sample, gla_sample, gmlp_v_sample)


_drawn_inputs = setup_inputs


def setup_inputs(seed=0):
    import zlib

    import numpy as np

    out = dict(_drawn_inputs(seed))
    spreads = {}
    factors = {'b_s': 8.0, 'gla_norm': 3.966, 'norm_ffn2': 3.879, 'norm_ple': 8.0}
    for name, (base, spread) in spreads.items():
        noise = np.random.default_rng([zlib.crc32(name.encode()), seed]).standard_normal(out[name].shape)
        drawn = base * np.exp(spread * noise) if base else spread * noise
        out[name] = __import__('jax').numpy.asarray(drawn.astype(out[name].dtype))
    for name, factor in factors.items():
        out[name] = (out[name] * factor).astype(out[name].dtype)
    return out
```

```python
from contextlib import ExitStack

import concourse.bass as bass
from concourse import mybir

P = 128
F32 = mybir.dt.float32
F32R = mybir.dt.float32r
ALU = mybir.AluOpType
ACT = mybir.ActivationFunctionType


def hybrid_trunk(nc, a, o):
    (y_prompt, y_sample, conv_prompt, gla_prompt, conv_sample, gla_sample, v_sample) = o
    depth, batch, seq, d_ple = a["p_prompt"].shape
    _, dec_batch, dec, d = a["x_sample"].shape[0:1] + a["x_sample"].shape[0:1] + a["x_sample"].shape[1:]
    assert depth == 1 and batch == 1 and dec_batch == 1
    ff = a["w_ffn1_gate"].shape[2]
    T = seq + dec
    KT = d // P
    FT = ff // P
    NB = 3
    TB = T // NB
    assert TB * NB == T and TB <= 512 and FT % 2 == 0
    NTILE = seq // P
    heads, dk, dv = a["state_gla"].shape[2:]
    L = 64
    NPAIR = heads // 2
    d_a = a["w_s"].shape[1] * 64
    rank = a["w_gate2"].shape[1]
    TAU = 16.0
    EPS = 1e-6
    D_C = heads * dv
    assert dec <= L and 2 * dk == P and dv == P and d_a == 2 * P

    COL_U, COL_VA, COL_B, COL_C, COL_X, COL_Q, COL_K, COL_V, COL_R = 0, 2, 4, 6, 8, 10, 12, 14, 18
    COL_GL = 22 * P

    PAIRS = FT // 2
    STEP = 6
    SET_A, SET_B = 0, 1
    uses = [0, 0]
    released = [[], []]
    done = []

    def take(s, counted=True):
        uses[s] += 1
        released[s].append((released[s] or [0])[-1] + counted)
        return s, uses[s] - 1

    def take_unit(use):
        done.append((use[0], use[1] + 1))
        return len(done) - 1

    class Ffn:

        def __init__(self):
            self.unit, self.a, self.b = len(done), uses[SET_A], uses[SET_B]
            for _ in range(PAIRS):
                for _ in range(2):
                    take_unit(take(SET_A))
                    take_unit(take(SET_B, counted=False))
                for _ in range(2):
                    tiles = [take((SET_A, SET_B)[j % 2]) for j in range(4)]
                    take_unit(tiles[3])

        def down(self, j, pair=PAIRS - 1):
            return j % 2, (self.a, self.b)[j % 2] + STEP * pair + 2 + j // 2

    ffn1 = Ffn()
    g_gl = take(SET_A)
    u_gl = take_unit(g_gl)
    g_va = [take(SET_B), take(SET_A)]
    u_va = [take_unit(g) for g in g_va]
    g_z = [take(SET_B), take(SET_A)]
    g_qkv = [take((SET_B, SET_A)[i % 2]) for i in range(8)]
    u_qkv = [take_unit(g) for g in g_qkv]
    g_big = [take(SET_A) for _ in range(NTILE + 1)]
    u_big = [take_unit(g) for g in g_big]
    g_r = g_big[NTILE:] + [take((SET_B, SET_A)[i % 2]) for i in range(3)]
    u_r = u_big[NTILE:] + [take_unit(g) for g in g_r[1:]]
    g_wo = [take((SET_A, SET_B)[j % 2]) for j in range(KT)]
    u_wo = [take_unit(g) for g in g_wo]
    ffn2 = Ffn()
    g_gate = [take(SET_A) for _ in range(KT)]
    g_proj = [take(SET_B, counted=False) for _ in range(KT)]
    u_ple = [take_unit(g) for g in g_gate]

    RELEASES = (STEP, STEP - 2)
    NROUND = 3
    N_STATE_OUT = 9

    def at_step(value, i, add=STEP):
        return value + add * i

    def used_up(n, i=0):
        if isinstance(i, int):
            n, i = n + STEP * i, 0
            return done[n - 2]
        s, count = done[n - 2 + STEP]
        return s, count - STEP + STEP * i

    ctx = ExitStack()
    with ctx:
        base = (nc.sbuf_base + 63) // 64 * 64
        top = [base]

        def at(name, shape, dt=F32, offset=None):
            n = 4
            for s in shape[1:]:
                n *= s
            if offset is None:
                offset = top[0]
                top[0] += (n + 31) // 32 * 32
            return nc.alloc_sbuf_tensor_at(name, shape, dt, offset=offset)

        x = at("x", [P, KT, T])
        late = x
        xh = at("xh", [P, KT, T], F32R)
        xl = at("xl", [P, KT, T], F32R)
        wst = [at(f"wst{b}", [P, KT, P]) for b in range(2)]
        wh = [at(f"wh{b}", [P, KT, P], F32R) for b in range(2)]
        wl = [at(f"wl{b}", [P, KT, P], F32R) for b in range(2)]
        r = at("r", [P, T])
        acc = at("acc", [P, T])
        ident = at("ident", [P, P])
        ones = at("ones", [P, P])
        rows = at("rows", [P, P])
        cols = at("cols", [P, 48])
        eps = at("eps", [P, 1])
        rcol = at("rcol", [P, 9])
        ricol = at("ricol", [P, 9])
        phase = top[0]
        hh = at("hh", [P, 2, T], F32R)
        hl = at("hl", [P, 2, T], F32R)
        tg = at("tg", [P, T])
        sg = at("sg", [P, T])
        sr = at("sr", [P, T])
        h32 = at("h32", [P, T])
        sq = at("sq", [P, 2, T])
        ple = top[0]
        pnat = at("pnat", [P, NTILE + 1, d_ple])
        p_t = at("p_t", [P, 2, T])
        wpst = at("wpst", [P, 2, d], offset=p_t.manual_sbuf_range[0])
        wph = at("wph", [P, 2, d], F32R)
        wpl = at("wpl", [P, 2, d], F32R)
        ffn_end = top[0]
        xin = at("xin", [P, NTILE, d], offset=ple)
        ffn_end = max(ffn_end, ple + NTILE * d * 4)
        xin_s = tg[:, 0:d]
        diag = sq[:, 0, :]
        top[0] = phase
        mix = at("mix", [P, 12, T])
        K_, KE, V_, VA, Q_ = 0, 2, 4, 8, 10
        st_a = at("st_a", [P, 10, P])
        st_q = at("st_q", [P, heads, P])
        ke_n = at("ke_n", [P, 2, 2 * P])
        v_n = at("v_n", [P, D_C])
        a_t = at("a_t", [P, heads, P])
        va_n = at("va_n", [P, d_a])
        ws_t = at("ws_t", [P, heads, P])
        bias = at("bias", [P, NPAIR, P])
        s0 = at("s0", [P, NPAIR, P])
        s1 = at("s1", [P, NPAIR, P])
        s_in = at("s_in", [P, NPAIR, P])
        decay = at("decay", [P, NPAIR, 2 * NTILE + 1])
        w2 = at("w2", [P, 2 * P])
        ln = at("ln", [P, 16])
        keep_hi = at("keep_hi", [P, P])
        keep_lo = at("keep_lo", [P, P])
        top[0] = max(top[0], ffn_end)
        assert top[0] <= nc.sbuf_usable_end, (top[0], nc.sbuf_usable_end)
        gl = st_a[0:rank].rearrange("p a b -> p (a b)")[:, 0:T]
        ws_in = st_q
        reset = acc
        flat = mix[:].rearrange("p a b -> p (a b)")
        ZW = T + 4
        zp = flat[:, 0:2 * ZW].rearrange("p (c t) -> p c t", c=2)
        cacc = flat[:, 2 * ZW:3 * ZW - 2]
        diag_o = st_a[:].rearrange("p a b -> p (a b)")[:, 0:T]
        r_gate = at("r_gate", [P, T], offset=ke_n.manual_sbuf_range[0])
        osq = acc
        assert ke_n.manual_sbuf_range[0] + T * 4 <= a_t.manual_sbuf_range[1] and 3 * ZW <= 4 * T

        ps = ctx.enter_context(nc.psum_tensor("ps", [P, 8, 512], F32))
        SETS = (0, 3)
        x_dram = nc.dram_tensor("x_spill", [P, KT, T], F32).ap()

        def sem(name):
            return ctx.enter_context(nc.semaphore(name))

        w_landed = [sem(f"w_landed{b}") for b in range(2)]
        w_hi = sem("w_hi")
        w_lo = sem("w_lo")
        full = [sem("full_a"), sem("full_b")]
        free = [sem("free_a"), sem("free_b")]
        up_block = sem("up_block")
        ones_set = sem("ones_set")
        mask_set = sem("mask_set")
        small_in = sem("small_in")
        x_in = [sem(f"x_in{i}") for i in range(3)]
        rows_t = sem("rows_t")
        cols_set = sem("cols_set")
        xt_full = sem("xt_full")
        xt_done = sem("xt_done")
        xg_hi = sem("xg_hi")
        xg_lo = sem("xg_lo")
        sq_set = sem("sq_set")
        sq_added = sem("sq_added")
        rs_cols = sem("rs_cols")
        rms_set = sem("rms_set")
        inv_set = sem("inv_set")
        diag_set = sem("diag_set")
        r_full = sem("r_full")
        r_set = sem("r_set")
        g_silu = sem("g_silu")
        g_silu_r = sem("g_silu_r")
        h_set = sem("h_set")
        h_hi = sem("h_hi")
        h_lo = sem("h_lo")
        spilled = sem("spilled")
        reloaded = sem("reloaded")
        ws_landed = sem("ws_landed")
        mix_in = sem("mix_in")
        ws_masked = sem("ws_masked")
        ws_full = sem("ws_full")
        ws_set = sem("ws_set")
        z_abs = sem("z_abs")
        z_exp = sem("z_exp")
        z_log = sem("z_log")
        ls_set = sem("ls_set")
        reset_set = sem("reset_set")
        g_cum = sem("g_cum")
        e_pos = sem("e_pos")
        e_neg = sem("e_neg")
        decay_set = sem("decay_set")
        e_r = sem("e_r")
        ke_set = sem("ke_set")
        zeroed = sem("zeroed")
        st_a_set = sem("st_a_set")
        st_q_set = sem("st_q_set")
        tile_t = sem("tile_t")
        a_full = sem("a_full")
        ds_full = sem("ds_full")
        gm_full = sem("gm_full")
        o_full = sem("o_full")
        v_n_set = sem("v_n_set")
        a_bounded = sem("a_bounded")
        a_masked = sem("a_masked")
        ke_n_set = sem("ke_n_set")
        ln_stat = sem("ln_stat")
        ln_mean = sem("ln_mean")
        ln_root = sem("ln_root")
        ln_inv = sem("ln_inv")
        va_n_set = sem("va_n_set")
        s1_set = sem("s1_set")
        s0_set = sem("s0_set")
        gm_set = sem("gm_set")
        o_set = sem("o_set")
        z_set = sem("z_set")
        conv_acc = sem("conv_acc")
        ya_set = sem("ya_set")
        yb_set = sem("yb_set")
        yc_set = sem("yc_set")
        osq_set = sem("osq_set")
        os_cols = sem("os_cols")
        orms_set = sem("orms_set")
        oinv_set = sem("oinv_set")
        odiag_set = sem("odiag_set")
        or_full = sem("or_full")
        o_normed = sem("o_normed")
        r_silu = sem("r_silu")
        y_hi = sem("y_hi")
        y_lo = sem("y_lo")
        p_in = sem("p_in")
        p_full = sem("p_full")
        p_copied = sem("p_copied")
        p_hi = sem("p_hi")
        p_lo = sem("p_lo")
        wp_hi = sem("wp_hi")
        wp_lo = sem("wp_lo")
        gate_sig = sem("gate_sig")
        ple_set = sem("ple_set")
        x_added = sem("x_added")
        gf_in = sem("gf_in")
        fin_full = sem("fin_full")
        fin_sq = sem("fin_sq")
        fin_root = sem("fin_root")
        fin_inv = sem("fin_inv")
        fin_set = sem("fin_set")
        outs = [sem(f"outs{i}") for i in range(2)]
        state_out = sem("state_out")

        block = ctx.enter_context(nc.Block())

        def banks(s):
            return ps[:, SETS[s]:SETS[s] + NB, 0:TB]

        def over_token_tiles(eng, body):
            body(0, 0)
            body(0, 1)
            with eng.Fori(1, NTILE // 2) as p:
                body(p, 0)
                body(p, 1)
            body(NTILE // 2, 0, dec)

        def y_of(k):
            return mix[:, (VA, VA + 1, Q_, Q_ + 1, V_, V_ + 1, V_ + 2, V_ + 3)[k], :]

        g_final = pnat[:].rearrange("p a b -> p (a b)")[:, 0:d]

        def y_out(t):
            return sq[:, t % 2, 0:d]

        def fin_ps(t):
            return ps[:, 2 * (t % 2):2 * (t % 2) + 2, :]

        def blocks(t):
            return t.rearrange("p (b n) -> p b n", b=NB)

        ROWS = [("norm_ffn1", KT), ("norm_mix", KT), ("norm_ffn2", KT), ("norm_ple", KT),
                ("gla_norm", heads), ("conv_w", 6), ("state_conv", 4), ("b_gate2", 2)]
        row_of, n_rows = {}, 0
        for name, n in ROWS:
            row_of[name] = n_rows
            n_rows += n
        assert n_rows <= 48
        GAIN = [row_of[n] for n in ("norm_ffn1", "norm_mix", "norm_ffn2", "norm_ple")]

        def gain(norm, j):
            return cols[:, GAIN[norm] + j:GAIN[norm] + j + 1]

        def late_weights(i):
            return (COL_B + i) if i < 6 else (COL_U + i - 6)

        def wait_used(eng, n, i=0):
            if isinstance(i, int) and n + STEP * i < 2:
                return
            s, count = used_up(n, i)
            eng.wait_ge(full[s], count)

        @block.sync
        def _(sp):
            def load(n, src, i=0, dst=None):
                b = n % 2
                if not (isinstance(i, int) and n + STEP * i < 2):
                    sp.wait_ge(w_lo, at_step(n - 1, i))
                sp.dma_start(wst[b][:] if dst is None else dst, src).then_inc(w_landed[b], 16)

            def column_tile(w, cs):
                return w[0, :, cs].rearrange("(k p) n -> p k n", p=P)

            def load_pair(f, wg, wu, wd, i):
                for q in range(2):
                    cs = bass.ds(i * 2 * P + q * P, P)
                    load(f.unit + 2 * q, column_tile(wg, cs), i)
                    load(f.unit + 2 * q + 1, column_tile(wu, cs), i)
                for half in range(2):
                    n = f.unit + 4 + half
                    src = wd[0, bass.ds(i * 2 * P, 2 * P), half * 4 * P:(half + 1) * 4 * P]
                    load(n, src.rearrange("(k p) n -> p k n", p=P), i,
                         wst[n % 2][:].rearrange("p (k q) n -> p k (q n)", k=2))

            ffn_w1 = (a["w_ffn1_gate"], a["w_ffn1_up"], a["w_ffn1_down"])
            ffn_w2 = (a["w_ffn2_gate"], a["w_ffn2_up"], a["w_ffn2_down"])

            for name, n in ROWS:
                v = a[name][0] if name != "state_conv" else a[name][0, 0]
                v = v.rearrange("w (c p) -> (w c) p", p=P) if len(v.shape) == 2 else \
                    v.rearrange("(c p) -> c p", p=P)
                sp.dma_start(rows[row_of[name]:row_of[name] + n, :], v).then_inc(small_in, 16)
            xp = a["x_prompt"][0].rearrange("(t p) d -> p t d", p=P)
            for g in range(2):
                sp.dma_start(xin[:, 4 * g:4 * g + 4, :], xp[:, 4 * g:4 * g + 4, :]).then_inc(x_in[g], 16)
            sp.dma_start(xin_s[0:dec, :], a["x_sample"][0]).then_inc(x_in[2], 16)
            load_pair(ffn1, *ffn_w1, 0)
            with sp.Fori(1, PAIRS) as i:
                load_pair(ffn1, *ffn_w1, i)

            load(u_gl, column_tile(a["w_in"], slice(COL_GL, COL_GL + rank)),
                 dst=wst[u_gl % 2][:, :, 0:rank])
            for j in (KT - 2, KT - 1):
                s, use = ffn1.down(j)
                sp.wait_ge(free[s], released[s][use])
            sp.dma_start(x_dram, x[:]).then_inc(spilled, 16)
            tiles = [COL_VA, COL_VA + 1, COL_Q, COL_Q + 1, COL_K, COL_K + 1, COL_V, COL_V + 1,
                     COL_V + 2, COL_V + 3] + [COL_B + i for i in range(6)] + [COL_U, COL_U + 1] + \
                    [COL_R + i for i in range(heads)]
            for i, c in enumerate(tiles):
                load(u_va[0] + i, column_tile(a["w_in"], slice(c * P, c * P + P)))
                if i == 0:
                    sp.wait_ge(rs_cols, 2)
                    sp.dma_start(w2[0:rank, :], a["w_gate2"][0]).then_inc(mix_in, 16)
                    for h in range(heads):
                        sp.dma_start(bias[64 * (h % 2):64 * (h % 2) + 64, h // 2, :],
                                     a["b_s"][0, h:h + 1, :].broadcast_to([64, P])).then_inc(mix_in, 16)
                    for e in range(2):
                        sp.dma_start(s_in[64 * e:64 * e + 64, :, :],
                                     a["state_gla"][0, 0].rearrange("(q e) k v -> e k q v", e=2)[e]
                                     ).then_inc(mix_in, 16)
                    sp.dma_start(ws_in[:], a["w_s"][0].rearrange("h i j -> i h j")).then_inc(ws_landed, 16)

            sp.wait_ge(s0_set, NTILE)
            sp.wait_ge(s1_set, NTILE + 1)
            sp.wait_ge(va_n_set, NTILE + 1)
            for dst, s in ((gla_prompt, s0), (gla_sample, s1)):
                for e in range(2):
                    sp.dma_start(dst[0, 0].rearrange("(q e) k v -> e k q v", e=2)[e],
                                 s[64 * e:64 * e + 64, :, :]).then_inc(state_out, 16)
            sp.dma_start(v_sample[0, 0], va_n[0:dec, :]).then_inc(state_out, 16)
            sp.wait_ge(z_set, 2)
            with nc.allow_non_contiguous_dma("two columns of z a stream, 1024 numbers in all"):
                for c in range(2):
                    for dst, end in ((conv_prompt, seq + 2), (conv_sample, ZW)):
                        sp.dma_start(dst[0, 0][:, c * P:c * P + P].rearrange("w p -> p w"),
                                     zp[:, c, end - 2:end]).then_inc(state_out, 16)
            for j in range(KT):
                load(u_wo[j], column_tile(a["w_o"], slice(j * P, j * P + P)))
                if j == 0:
                    sp.wait_ge(ya_set, 2)
                    sp.wait_ge(yb_set, 2)
                    sp.wait_ge(spilled, 16)
                    sp.dma_start(x[:], x_dram).then_inc(reloaded, 16)
            load_pair(ffn2, *ffn_w2, 0)
            sp.wait_ge(y_lo, KT)
            sp.wait_ge(state_out, 16 * N_STATE_OUT)
            sp.dma_start(pnat[:, 0:NTILE, :], a["p_prompt"][0, 0].rearrange("(t p) c -> p t c", p=P)
                         ).then_inc(p_in, 16)
            sp.dma_start(pnat[0:dec, NTILE, :], a["p_sample"][0, 0]).then_inc(p_in, 16)
            sp.dma_start(wpst[:], a["w_ple_proj"][0].rearrange("(k p) n -> p k n", p=P)).then_inc(p_in, 16)
            with sp.Fori(1, PAIRS) as i:
                load_pair(ffn2, *ffn_w2, i)
            for j in range(KT):
                load(u_ple[j], column_tile(a["w_ple_gate"], slice(j * P, j * P + P)))
                if j == 0:
                    sp.wait_ge(p_copied, NROUND)
                    sp.dma_start(g_final, a["final_norm"].rearrange("(o n) -> o n", o=1)
                                 .broadcast_to([P, d])).then_inc(gf_in, 16)
            for t in range(NTILE + 1):
                sp.wait_ge(fin_set, t + 1)
                if t < NTILE:
                    sp.dma_start(y_prompt[0, t * P:t * P + P, :], y_out(t)).then_inc(outs[t % 2], 16)
                else:
                    sp.dma_start(y_sample[0], y_out(t)[P - dec:P]).then_inc(outs[t % 2], 16)
            for b in range(2):
                sp.wait_ge(outs[b], 16 * ((NTILE + 2 - b) // 2))
            sp.wait_ge(state_out, 16 * N_STATE_OUT)

        @block.gpsimd
        def _(pool):
            def add_squares(norm):
                for j in range(1, KT):
                    pool.wait_ge(sq_set, KT * norm + j + 1)
                    if j > 1:
                        pool.wait_ge(sq_added, (KT - 1) * norm + j - 1)
                    pool.tensor_tensor(acc[:], acc[:], sq[:, j % 2, :], ALU.add).then_inc(sq_added, 1)

            def silu_times_r(n_silu, n_h):
                pool.wait_ge(g_silu, n_silu)
                if n_h is not None:
                    pool.wait_ge(h_set, n_h)
                pool.tensor_tensor(sr[:], sg[:], r[:], ALU.mult).then_inc(g_silu_r, 1)

            def ffn_pairs(before):
                def pair(i):
                    n = before + i
                    first = isinstance(n, int) and n == 0
                    silu_times_r(n * 2 + 1, None if first else n * (1 + NB))
                    silu_times_r(n * 2 + 2, n * (1 + NB) + 1)
                pair(0)
                with pool.Fori(1, PAIRS) as i:
                    pair(i)

            pool.memset(ones[:], 1.0).then_inc(ones_set, 1)
            pool.memset(eps[:], EPS).then_inc(ones_set, 1)
            pool.memset(ident[:], 0.0).then_inc(ones_set, 1)
            pool.wait_ge(ones_set, 3)
            pool.affine_select(out=ident[:], in_=ident[:], compare_op=ALU.not_equal, fill=1.0, base=0,
                               pattern=[[-1, P]], channel_multiplier=1).then_inc(ones_set, 1)

            ffn_pairs(0)
            add_squares(1)

            pool.wait_ge(rs_cols, 2)
            pool.memset(reset[:], 1.0).then_inc(reset_set, 1)
            pool.wait_ge(reset_set, 1)
            pool.memset(reset[:].rearrange("p (b n) -> p b n", n=dec)[:, 0:T // dec:L // dec, 0:1], 0.0
                        ).then_inc(reset_set, 1)
            for m, big in ((keep_hi, 3e38), (keep_lo, -3e38)):
                pool.memset(m[:], big).then_inc(mask_set, 1)
            pool.wait_ge(mask_set, 2)
            for m in (keep_hi, keep_lo):
                pool.memset(m[0:L, L:P], 0.0).then_inc(mask_set, 1)
            pool.wait_ge(mask_set, 4)
            for m in (keep_hi, keep_lo):
                pool.affine_select(out=m[:], in_=m[:], compare_op=ALU.is_ge, fill=0.0, base=0,
                                   pattern=[[1, P]], channel_multiplier=-1).then_inc(mask_set, 1)
            pool.wait_ge(ws_landed, 16)
            pool.memset(ws_in[0:L, :, L:P], 0.0).then_inc(ws_masked, 1)
            pool.memset(ke_n[:], 0.0).then_inc(zeroed, 1)
            pool.memset(s0[:], 0.0).then_inc(zeroed, 1)
            for c in range(NPAIR):
                pool.wait_ge(e_pos, c + 1)
                pool.tensor_copy(decay[:, c, 0:2 * NTILE], mix[:, Q_ + c, L - 1:seq:L])
                pool.tensor_copy(decay[:, c, 2 * NTILE:2 * NTILE + 1], mix[:, Q_ + c, T - 1:T]
                                 ).then_inc(decay_set, 1)
                pool.wait_ge(decay_set, c + 1)
                pool.tensor_tensor(mix[:, Q_ + c, :], mix[:, Q_ + c, :], r[:], ALU.mult).then_inc(e_r, 1)
                pool.wait_ge(e_neg, c + 1)
                pool.tensor_tensor(mix[:, K_ + c, :], mix[:, K_ + c, :], r[:], ALU.mult).then_inc(e_r, 1)
            pool.wait_ge(ws_full, 1)
            pool.memset(st_q[:], 0.0).then_inc(zeroed, 1)
            pool.wait_ge(g_cum, 2)
            pool.wait_ge(ke_set, NPAIR)
            pool.wait_ge(free[SET_A], released[SET_A][g_qkv[7][1]])

            def mixers(p, e, w=P):
                t = 2 * p + e
                tok = bass.ds(t * P, w)
                first = isinstance(t, int) and t == 0
                if not first:
                    pool.wait_ge(a_full, t)
                pool.tensor_copy(st_a[:, :, 0:w], mix[:, 0:10, tok]).then_inc(st_a_set, 1)

            over_token_tiles(pool, mixers)

            pool.wait_ge(a_full, NTILE + 1)
            pool.wait_ge(free[SET_A], released[SET_A][g_big[NTILE - 1][1]])
            for c in range(2):
                pool.memset(zp[:, c, 0:2], 0.0)
                first = row_of["state_conv"] + c
                pool.tensor_copy(zp[:, c, seq + 2:seq + 4], cols[:, first:first + 3:2])
                pool.tensor_tensor(zp[:, c, 2:seq + 2], late[:, 2 + c, 0:seq], late[:, 4 + c, 0:seq],
                                   ALU.mult)
                pool.tensor_tensor(zp[:, c, seq + 4:ZW], late[:, 2 + c, seq:T], late[:, 4 + c, seq:T],
                                   ALU.mult).then_inc(z_set, 1)
            pool.wait_ge(gm_set, NTILE + 1)
            for c in range(2):
                pool.tensor_tensor(mix[:, VA + c, :], mix[:, VA + c, :], late[:, 6 + c, :], ALU.mult
                                   ).then_inc(ya_set, 1)

            def y_b(c):
                pool.wait_ge(conv_acc, 3 * c + 3)
                pool.tensor_tensor(mix[:, Q_ + c, 0:seq], cacc[:, 0:seq], late[:, c, 0:seq], ALU.mult)
                pool.tensor_tensor(mix[:, Q_ + c, seq:T], cacc[:, seq + 2:T + 2], late[:, c, seq:T],
                                   ALU.mult).then_inc(yb_set, 1)

            def y_c(h):
                pool.wait_ge(r_silu, h + 1)
                pool.wait_ge(o_normed, 2 * h + 2)
                pool.tensor_tensor(mix[:, V_ + h, :], mix[:, V_ + h, :], r_gate[:], ALU.mult
                                   ).then_inc(yc_set, 1)

            y_b(0)
            y_c(0)
            y_b(1)
            for h in range(1, heads):
                y_c(h)
            add_squares(2)
            ffn_pairs(PAIRS)
            add_squares(3)
            for j in range(KT):
                pool.wait_ge(ple_set, j + 1)
                pool.tensor_tensor(x[:, j, :], x[:, j, :], h32[:], ALU.add).then_inc(x_added, 1)

        @block.scalar
        def _(act):
            def split_hi(n, i=0, width=P):
                b = n % 2
                act.wait_ge(w_landed[b], 16 * (n // 2 + 1 + STEP // 2 * i))
                wait_used(act, n, i)
                act.activation(wh[b][:, :, 0:width], wst[b][:, :, 0:width], ACT.Copy).then_inc(w_hi, 1)

            def x_hi(norm, j):
                act.activation(xh[:, j, :], x[:, j, :], ACT.Copy, scale=gain(norm, j)).then_inc(xg_hi, 1)

            def square(norm, j):
                if j == 0 and norm > 0:
                    act.wait_ge(rs_cols, norm)
                if j > 2:
                    act.wait_ge(sq_added, (KT - 1) * norm + j - 2)
                act.activation(acc[:] if j == 0 else sq[:, j % 2, :], x[:, j, :], ACT.Square
                               ).then_inc(sq_set, 1)

            def finish_norm(norm):
                act.wait_ge(rs_cols, norm + 1)
                act.activation(rcol[:, 0:NTILE], ps[:, 6, 0:NTILE], ACT.Sqrt, bias=eps[:], scale=1.0 / d)
                act.activation(rcol[0:dec, NTILE:NTILE + 1], ps[0:dec, 6, NTILE:NTILE + 1], ACT.Sqrt,
                               bias=eps[0:dec], scale=1.0 / d).then_inc(rms_set, 1)
                act.wait_ge(r_full, 2 * norm + 1)
                act.activation(r[:, 0:seq].rearrange("p (b n) -> p b n", b=2), ps[:, 6:8, :], ACT.Copy
                               ).then_inc(r_set, 1)
                act.wait_ge(r_full, 2 * norm + 2)
                act.activation(r[:, seq:T], ps[:, 6, 0:dec], ACT.Copy).then_inc(r_set, 1)

            def silu(f, q, i, k):
                act.wait_ge(free[SET_A], at_step(released[SET_A][f.a + q], i))
                if not (isinstance(k, int) and k == 0):
                    act.wait_ge(g_silu_r, k)
                act.activation(sg[:], tg[:], ACT.Silu).then_inc(g_silu, 1)

            def h_part(n, q, cols_):
                act.wait_ge(h_set, n)
                act.activation(hh[:, q, cols_], h32[:, cols_], ACT.Copy).then_inc(h_hi, 1)

            def ffn(f, before, norm, extra=None):
                def pair(i, first=False, last=False):
                    n = f.unit
                    k = before + i
                    split_hi(n + 1, i)
                    if first:
                        finish_norm(norm)
                    if last and extra:
                        extra()
                    silu(f, 0, i, 2 * k)
                    split_hi(n + 2, i)
                    h_part((1 + NB) * k + 1, 0, slice(0, T))
                    split_hi(n + 3, i)
                    silu(f, 1, i, 2 * k + 1)
                    split_hi(n + 4, i)
                    for blk in range(NB):
                        h_part((1 + NB) * k + 2 + blk, 1, slice(blk * TB, blk * TB + TB))
                    split_hi(n + 5, i)
                    for j in range(KT if last else 0):
                        if j == KT // 2:
                            split_hi(n + 6, i, rank if norm == 0 else P)
                        s, use = f.down(j)
                        act.wait_ge(free[s], released[s][use])
                        square(norm + 1, j)
                        x_hi(norm + 1, j)
                    if not last:
                        split_hi(n + 6, i)
                return pair

            def p_copies():
                for g in range(NROUND):
                    act.wait_ge(p_full, g + 1)
                    w = min(4 * P, T - 4 * P * g)
                    act.activation(p_t[:, :, 4 * P * g:4 * P * g + w], ps[:, 6:8, 0:w], ACT.Copy
                                   ).then_inc(p_copied, 1)

            act.wait_ge(cols_set, 1)
            act.wait_ge(xt_done, NTILE + 1)
            for j in range(KT):
                x_hi(0, j)
                if j == 0:
                    split_hi(ffn1.unit)
            for j in range(KT):
                square(0, j)
            pair = ffn(ffn1, 0, 0)
            pair(0, first=True)
            with act.Fori(1, PAIRS - 1) as i:
                pair(i)
            pair(PAIRS - 1, last=True)

            split_hi(u_va[0])
            finish_norm(1)
            split_hi(u_va[1])
            split_hi(u_qkv[0])
            split_hi(u_qkv[1])
            for c in range(NPAIR):
                s, use = g_z[c]
                act.wait_ge(full[s], use + 1)
                act.activation(mix[:, KE + c, :].rearrange("p (b n) -> p b n", b=NB), banks(s), ACT.Abs,
                               bias=cols[:, row_of["b_gate2"] + c:row_of["b_gate2"] + c + 1]
                               ).then_inc(z_abs, 1)
            for c in range(NPAIR):
                act.wait_ge(z_abs, c + 1)
                act.activation(mix[:, KE + c, :], mix[:, KE + c, :], ACT.Exp, scale=-1.0).then_inc(z_exp, 1)
                act.wait_ge(z_exp, c + 1)
                act.activation(mix[:, KE + c, :], mix[:, KE + c, :], ACT.Ln, bias=ones[:, 0:1]
                               ).then_inc(z_log, 1)
            split_hi(u_qkv[2])
            for c in range(NPAIR):
                act.wait_ge(g_cum, c + 1)
                act.activation(mix[:, Q_ + c, :], mix[:, KE + c, :], ACT.Exp, scale=1.0 / TAU
                               ).then_inc(e_pos, 1)
                act.activation(mix[:, K_ + c, :], mix[:, KE + c, :], ACT.Exp, scale=-1.0 / TAU
                               ).then_inc(e_neg, 1)
            for u in u_qkv[3:]:
                split_hi(u)
            split_hi(u_big[0])

            def mixers(p, e, w=P):
                t = 2 * p + e
                first = isinstance(t, int) and t == 0
                if first:
                    act.wait_ge(zeroed, 3)
                    act.wait_ge(free[SET_B], released[SET_B][g_qkv[0][1]])
                    act.wait_ge(free[SET_A], released[SET_A][g_qkv[1][1]])
                else:
                    act.wait_ge(o_full, t)
                for m in range(2):
                    last = act.activation(st_q[64 * m:64 * m + 64, m:heads:2, 0:w],
                                          mix[64 * m:64 * m + 64, Q_:Q_ + 2, bass.ds(t * P, w)], ACT.Copy)
                last.then_inc(st_q_set, 1)
                n = u_big[0] + 1 + e
                act.wait_ge(w_landed[n % 2], 16 * (n // 2 + 1 + p))
                act.wait_ge(full[SET_A], g_big[0][1] + t)
                act.activation(wh[n % 2][:], wst[n % 2][:], ACT.Copy).then_inc(w_hi, 1)
                act.wait_ge(tile_t, t + 1)
                if not first:
                    act.wait_ge(o_full, t)
                act.activation(v_n[0:w, :], ps[0:w, 3, :], ACT.Copy).then_inc(v_n_set, 1)
                act.wait_ge(ln_mean, t + 1)
                act.activation(ln[0:w, 8:9], ln[0:w, 7:8], ACT.Sqrt, bias=eps[0:w]).then_inc(ln_root, 1)
                act.wait_ge(o_full, t + 1)
                act.activation(mix[:, V_:V_ + heads, bass.ds(t * P, w)],
                               ps[:, 6, :].rearrange("p (h i) -> p h i", h=heads)[:, :, 0:w], ACT.Copy
                               ).then_inc(o_set, 1)

            over_token_tiles(act, mixers)

            def o_square(h):
                if h > 0:
                    act.wait_ge(os_cols, h)
                act.activation(osq[:], mix[:, V_ + h, :], ACT.Square).then_inc(osq_set, 1)

            def o_root(h):
                act.wait_ge(os_cols, h + 1)
                if h > 0:
                    act.wait_ge(oinv_set, h)
                act.activation(rcol[:, 0:NTILE], ps[:, 6, 0:NTILE], ACT.Sqrt, bias=eps[:], scale=1.0 / dv)
                act.activation(rcol[0:dec, NTILE:NTILE + 1], ps[0:dec, 6, NTILE:NTILE + 1], ACT.Sqrt,
                               bias=eps[0:dec], scale=1.0 / dv).then_inc(orms_set, 1)

            def gate_silu(h):
                s, use = g_r[h]
                act.wait_ge(free[s], released[s][use])
                act.activation(r_gate[:], r_gate[:], ACT.Silu).then_inc(r_silu, 1)

            def y_part(k):
                if k == 0:
                    act.wait_ge(full[g_r[3][0]], g_r[3][1] + 1)
                if k < 2:
                    act.wait_ge(ya_set, k + 1)
                elif k < 4:
                    act.wait_ge(yb_set, k - 1)
                else:
                    act.wait_ge(yc_set, k - 3)
                act.activation(xh[:, k, :], y_of(k), ACT.Copy).then_inc(y_hi, 1)

            act.wait_ge(o_set, NTILE + 1)
            act.wait_ge(g_cum, 2)
            o_square(0)
            o_root(0)
            split_hi(u_r[2])
            o_square(1)
            gate_silu(0)
            o_root(1)
            split_hi(u_r[3])
            o_square(2)
            o_root(2)
            gate_silu(1)
            split_hi(u_wo[0])
            o_square(3)
            o_root(3)
            gate_silu(2)
            y_part(0)
            y_part(1)
            gate_silu(3)
            split_hi(u_wo[1])
            for k in range(2, KT):
                y_part(k)

            for j in range(KT):
                if j < KT - 1:
                    if j > 0:
                        split_hi(u_wo[j + 1])
                else:
                    split_hi(ffn2.unit)
                s, use = g_wo[j]
                act.wait_ge(free[s], released[s][use])
                square(2, j)
            for j in range(KT):
                x_hi(2, j)
            pair = ffn(ffn2, PAIRS, 2, p_copies)
            pair(0, first=True)
            act.wait_ge(p_in, 48)
            act.activation(wph[:], wpst[:], ACT.Copy).then_inc(wp_hi, 1)
            with act.Fori(1, PAIRS - 1) as i:
                pair(i)
            pair(PAIRS - 1, last=True)

            for c in range(2):
                act.activation(hh[:, c, :], p_t[:, c, :], ACT.Copy).then_inc(p_hi, 1)
            for j in range(KT):
                if j < KT - 1:
                    split_hi(u_ple[j + 1])
                if j == 0:
                    finish_norm(3)
                act.wait_ge(free[SET_A], released[SET_A][g_gate[j][1]])
                if j > 0:
                    act.wait_ge(ple_set, j)
                act.activation(sg[:], tg[:], ACT.Sigmoid).then_inc(gate_sig, 1)

            for t in range(NTILE + 1):
                rs = slice(0, P) if t < NTILE else slice(P - dec, P)
                act.wait_ge(fin_full, t + 1)
                if t > 0:
                    act.wait_ge(fin_inv, t)
                act.activation(tg[rs, 0:d], fin_ps(t)[rs], ACT.Square, accum_out=rcol[rs, 0:1]
                               ).then_inc(fin_sq, 1)
                act.wait_ge(fin_sq, t + 1)
                act.activation(rcol[rs, 1:2], rcol[rs, 0:1], ACT.Sqrt, bias=eps[rs], scale=1.0 / d
                               ).then_inc(fin_root, 1)

        @block.vector
        def _(dve):
            def split_lo(n, i=0, width=P):
                b = n % 2
                dve.wait_ge(w_hi, at_step(n + 1, i))
                dve.tensor_tensor(wl[b][:, :, 0:width], wst[b][:, :, 0:width],
                                  wh[b][:, :, 0:width].bitcast(F32), ALU.subtract).then_inc(w_lo, 1)

            def x_lo(norm, j):
                dve.wait_ge(xg_hi, KT * norm + j + 1)
                dve.scalar_tensor_tensor(xl[:, j, :], x[:, j, :], gain(norm, j), xh[:, j, :].bitcast(F32),
                                         ALU.mult, ALU.subtract).then_inc(xg_lo, 1)

            def on_diagonals(dg, n_set):
                dve.reciprocal(ricol[:, 0:NTILE], rcol[:, 0:NTILE])
                dve.reciprocal(ricol[0:dec, NTILE:NTILE + 1], rcol[0:dec, NTILE:NTILE + 1]).then_inc(*n_set[0])
                dve.wait_ge(*n_set[1])
                dve.tensor_tensor(dg[:, 0:seq].rearrange("p (t n) -> p t n", n=P),
                                  ident[:].unsqueeze(1).broadcast_to([P, NTILE, P]),
                                  ricol[:, 0:NTILE].unsqueeze(2).broadcast_to([P, NTILE, P]), ALU.mult)
                dve.tensor_scalar(dg[0:dec, seq:T], ident[0:dec, 0:dec], ricol[0:dec, NTILE:NTILE + 1],
                                  None, ALU.mult).then_inc(*n_set[2])

            def finish_norm(norm):
                dve.wait_ge(rms_set, norm + 1)
                on_diagonals(diag, ((inv_set, 1), (inv_set, norm + 1), (diag_set, 1)))

            def ffn(f, before, norm):
                def pair(i, first=False, last=False):
                    n = f.unit
                    k = before + i
                    nh = (1 + NB) * k

                    def scale_gate(q):
                        dve.wait_ge(full[SET_A], at_step(f.a + q + 1, i))
                        if not (isinstance(k, int) and k == 0 and q == 0):
                            dve.wait_ge(g_silu, 2 * k + q)
                        dve.tensor_tensor(blocks(tg[:]), banks(SET_A), blocks(r[:]), ALU.mult
                                          ).then_inc(free[SET_A], 1)

                    def h_lo_part(m, q, cs):
                        dve.wait_ge(h_hi, nh + m)
                        dve.tensor_tensor(hl[:, q, cs], h32[:, cs], hh[:, q, cs].bitcast(F32),
                                          ALU.subtract).then_inc(h_lo, 1)

                    split_lo(n + 1, i)
                    if first:
                        finish_norm(norm)
                        dve.wait_ge(r_set, 2 * norm + 2)
                    scale_gate(0)
                    split_lo(n + 2, i)
                    dve.wait_ge(full[SET_B], at_step(f.b + 1, i))
                    dve.wait_ge(g_silu_r, 2 * k + 1)
                    dve.tensor_tensor(blocks(h32[:]), banks(SET_B), blocks(sr[:]), ALU.mult
                                      ).then_inc(h_set, 1)
                    split_lo(n + 3, i)
                    h_lo_part(1, 0, slice(0, T))
                    scale_gate(1)
                    split_lo(n + 4, i)
                    for blk in range(NB):
                        cs = slice(blk * TB, blk * TB + TB)
                        if blk < NB - 1:
                            dve.wait_ge(up_block, (NB - 1) * k + blk + 1)
                        else:
                            dve.wait_ge(full[SET_B], at_step(f.b + 2, i))
                        if blk == 0:
                            dve.wait_ge(g_silu_r, 2 * k + 2)
                        dve.tensor_tensor(h32[:, cs], ps[:, SETS[SET_B] + blk, 0:TB], sr[:, cs], ALU.mult
                                          ).then_inc(h_set, 1)
                        h_lo_part(2 + blk, 1, cs)
                    split_lo(n + 5, i)
                    for j in range(KT):
                        if j == KT // 2:
                            split_lo(n + 6, i, rank if last and norm == 0 else P)
                        s = j % 2
                        dve.wait_ge(full[s], at_step((f.a, f.b)[s] + 3 + j // 2, i))
                        if i is not None and not first:
                            dve.wait_ge(free[s], at_step(released[s][f.down(j, 0)[1]] - RELEASES[s], i,
                                                         RELEASES[s]))
                        dve.scalar_tensor_tensor(blocks(x[:, j, :]), banks(s), 0.5, blocks(x[:, j, :]),
                                                 ALU.mult, ALU.add).then_inc(free[s], 1)
                        if last and j > 0:
                            x_lo(norm + 1, j - 1)
                    if last:
                        x_lo(norm + 1, KT - 1)
                return pair

            dve.wait_ge(rows_t, 1)
            dve.tensor_copy(cols[:], ps[:, 7, 0:n_rows]).then_inc(cols_set, 1)
            for t in range(NTILE + 1):
                w = P if t < NTILE else dec
                dve.wait_ge(xt_full, t + 1)
                dve.tensor_copy(x[:, :, t * P:t * P + w],
                                ps[:, 2 * (t % 2):2 * (t % 2) + 2, :].rearrange("p b (j n) -> p (b j) n", n=P)
                                [:, :, 0:w]).then_inc(xt_done, 1)
            for j in range(KT):
                x_lo(0, j)
                if j == 0:
                    split_lo(ffn1.unit)
            for j in range(1, KT):
                dve.wait_ge(sq_set, j + 1)
                if j > 1:
                    dve.wait_ge(sq_added, j - 1)
                dve.tensor_tensor(acc[:], acc[:], sq[:, j % 2, :], ALU.add).then_inc(sq_added, 1)
            pair = ffn(ffn1, 0, 0)
            pair(0, first=True)
            with dve.Fori(1, PAIRS - 1) as i:
                pair(i)
            pair(PAIRS - 1, last=True)

            def result(use):
                s, u = use
                dve.wait_ge(full[s], u + 1)
                return banks(s)

            def keep(use, slot):
                src = result(use)
                dve.tensor_tensor(blocks(mix[:, slot, :]), src, blocks(r[:]), ALU.mult
                                  ).then_inc(free[use[0]], 1)

            split_lo(u_va[0])
            finish_norm(1)
            split_lo(u_va[1])
            dve.wait_ge(r_set, 4)
            s, use = g_gl
            dve.wait_ge(full[s], use + 1)
            dve.tensor_tensor(blocks(gl), banks(s)[0:rank], blocks(r[0:rank]), ALU.mult
                              ).then_inc(free[s], 1)
            split_lo(u_qkv[0])
            keep(g_va[0], VA)
            keep(g_va[1], VA + 1)
            split_lo(u_qkv[1])
            dve.wait_ge(ws_full, 1)
            dve.tensor_copy(ws_t[:], ps[:, 6, :].rearrange("p (h i) -> p h i", h=heads)).then_inc(ws_set, 1)
            for c in range(NPAIR):
                s, use = g_z[c]
                dve.wait_ge(z_abs, c + 1)
                dve.tensor_scalar(blocks(mix[:, K_ + c, :]), banks(s),
                                  cols[:, row_of["b_gate2"] + c:row_of["b_gate2"] + c + 1], 0.0,
                                  ALU.add, ALU.min).then_inc(free[s], 1)
            dve.wait_ge(reset_set, 2)
            for c in range(NPAIR):
                s, use = g_z[c]
                dve.wait_ge(z_log, c + 1)
                dve.wait_ge(free[s], released[s][use])
                dve.tensor_tensor(mix[:, K_ + c, :], mix[:, K_ + c, :], mix[:, KE + c, :], ALU.subtract
                                  ).then_inc(ls_set, 1)
                dve.wait_ge(ls_set, c + 1)
                dve.tensor_tensor_scan(mix[:, KE + c, :], reset[:], mix[:, K_ + c, :], 0.0,
                                       ALU.mult, ALU.add).then_inc(g_cum, 1)
            split_lo(u_qkv[2])
            for c in range(NPAIR):
                dve.wait_ge(e_r, 2 * c + 1)
                src = result(g_qkv[c])
                dve.scalar_tensor_tensor(blocks(mix[:, Q_ + c, :]), src, float(dk) ** -0.5,
                                         blocks(mix[:, Q_ + c, :]), ALU.mult, ALU.mult
                                         ).then_inc(free[g_qkv[c][0]], 1)
                split_lo(u_qkv[3 + c])
            for c in range(NPAIR):
                dve.wait_ge(e_r, 2 * c + 2)
                s, use = g_qkv[2 + c]
                src = result(g_qkv[2 + c])
                dve.tensor_tensor(blocks(mix[:, K_ + c, :]), src, blocks(mix[:, K_ + c, :]), ALU.mult
                                  ).then_inc(free[s], 1)
                dve.wait_ge(free[s], released[s][use])
                dve.tensor_tensor(mix[:, KE + c, 0:seq].rearrange("p (b n) -> p b n", n=L),
                                  mix[:, K_ + c, 0:seq].rearrange("p (b n) -> p b n", n=L),
                                  decay[:, c, 0:2 * NTILE].unsqueeze(2).broadcast_to([P, 2 * NTILE, L]),
                                  ALU.mult)
                dve.tensor_scalar(mix[:, KE + c, seq:T], mix[:, K_ + c, seq:T],
                                  decay[:, c, 2 * NTILE:2 * NTILE + 1], None, ALU.mult).then_inc(ke_set, 1)
                split_lo(u_qkv[5 + c])
            for v in range(heads):
                keep(g_qkv[4 + v], V_ + v)
                if v == 0:
                    split_lo(u_qkv[7])
                if v == 1:
                    split_lo(u_big[0])

            def mixers(p, e, w=P):
                t = 2 * p + e
                first = isinstance(t, int) and t == 0
                sample = w < P
                nblk = 1 if sample else 2
                n = u_big[0] + 1 + e
                dve.wait_ge(w_hi, n + 1 + 2 * p)
                dve.tensor_tensor(wl[n % 2][:], wst[n % 2][:], wh[n % 2][:].bitcast(F32), ALU.subtract
                                  ).then_inc(w_lo, 1)
                va = ps[0:w, 4, 2 * P:4 * P]
                dve.wait_ge(tile_t, t + 1)
                if not first:
                    dve.wait_ge(va_n_set, t)
                dve.bn_stats(ln[0:w, 0:6], va).then_inc(ln_stat, 1)
                if first:
                    dve.wait_ge(zeroed, 2)
                else:
                    dve.wait_ge(ds_full, t)
                dve.wait_ge(ln_stat, t + 1)
                for m in range(nblk):
                    rs = slice(L * m, min(L * m + L, w))
                    last = dve.tensor_copy(ke_n[rs, m, :], ps[rs, 4, 0:2 * P])
                last.then_inc(ke_n_set, 1)
                dve.bn_aggr(ln[0:w, 6:8], ln[0:w, 0:6]).then_inc(ln_mean, 1)
                dve.wait_ge(ln_root, t + 1)
                dve.reciprocal(ln[0:w, 9:10], ln[0:w, 8:9]).then_inc(ln_inv, 1)
                dve.wait_ge(ln_inv, t + 1)
                if not first:
                    dve.wait_ge(gm_full, t)
                dve.tensor_scalar(va_n[0:w, :], va, ln[0:w, 6:7], ln[0:w, 9:10], ALU.subtract, ALU.mult
                                  ).then_inc(va_n_set, 1)
                if not first:
                    dve.wait_ge(o_full, t)
                dve.wait_ge(a_full, t + 1)
                dve.tensor_tensor(a_t[0:w, :, 0:w],
                                  ps[:, 5, :].rearrange("p (h i) -> p h i", h=heads)[0:w, :, 0:w],
                                  keep_hi[0:w, 0:w].unsqueeze(1).broadcast_to([w, heads, w]), ALU.min
                                  ).then_inc(a_bounded, 1)
                dve.wait_ge(a_bounded, t + 1)
                dve.tensor_tensor(a_t[0:w, :, 0:w], a_t[0:w, :, 0:w],
                                  keep_lo[0:w, 0:w].unsqueeze(1).broadcast_to([w, heads, w]), ALU.max
                                  ).then_inc(a_masked, 1)
                before = s_in if sample else s0
                dve.wait_ge(ds_full, t + 1)
                if not first:
                    dve.wait_ge(o_full, t)
                    dve.wait_ge(s0_set, min(t, NTILE) if isinstance(t, int) else t)
                for c in range(NPAIR):
                    last = dve.scalar_tensor_tensor(s1[:, c, :], before[:, c, :],
                                                    decay[:, c, bass.ds(2 * t, 1)],
                                                    ps[:, 7, c * P:c * P + P], ALU.mult, ALU.add)
                last.then_inc(s1_set, 1)
                dve.wait_ge(gm_full, t + 1)
                dve.tensor_tensor(mix[:, VA:VA + 2, bass.ds(t * P, w)],
                                  ps[:, 3, 0:2 * P].rearrange("p (c n) -> p c n", c=2)[:, :, 0:w],
                                  bias[:, :, 0:w], ALU.add).then_inc(gm_set, 1)
                if not sample:
                    dve.wait_ge(o_full, t + 1)
                    dve.wait_ge(s1_set, t + 1)
                    for c in range(NPAIR):
                        last = dve.scalar_tensor_tensor(s0[:, c, :], s1[:, c, :],
                                                        decay[:, c, bass.ds(2 * t + 1, 1)],
                                                        ps[:, 7, 2 * P + c * P:3 * P + c * P],
                                                        ALU.mult, ALU.add)
                    last.then_inc(s0_set, 1)
                    dve.wait_ge(full[SET_A], g_big[0][1] + 1 + t)
                    dve.tensor_tensor(blocks(late[:, bass.ds(t, 1), :].rearrange("p a n -> p (a n)")),
                                      banks(SET_A), blocks(r[:]), ALU.mult).then_inc(free[SET_A], 1)

            dve.wait_ge(spilled, 16)
            dve.wait_ge(mix_in, 16 * 7)
            dve.wait_ge(mask_set, 6)
            over_token_tiles(dve, mixers)

            def scale_r(h):
                src = result(g_r[h])
                if h > 0:
                    dve.wait_ge(yc_set, h)
                else:
                    dve.wait_ge(o_full, NTILE + 1)
                dve.tensor_tensor(blocks(r_gate[:]), src, blocks(r[:]), ALU.mult
                                  ).then_inc(free[g_r[h][0]], 1)

            def o_invert(h):
                dve.wait_ge(orms_set, h + 1)
                if h > 0:
                    dve.wait_ge(or_full, 2 * h)
                on_diagonals(diag_o, ((oinv_set, 1), (oinv_set, h + 1), (odiag_set, 1)))

            def o_norm(h):
                g = cols[:, row_of["gla_norm"] + h:row_of["gla_norm"] + h + 1]
                dve.wait_ge(or_full, 2 * h + 1)
                o_ = mix[:, V_ + h, 0:seq].rearrange("p (b n) -> p b n", b=2)
                dve.scalar_tensor_tensor(o_, ps[:, 6:8, :], g, o_, ALU.mult, ALU.mult).then_inc(o_normed, 1)
                dve.wait_ge(or_full, 2 * h + 2)
                o_ = mix[:, V_ + h, seq:T]
                dve.scalar_tensor_tensor(o_, ps[:, 6, 0:dec], g, o_, ALU.mult, ALU.mult
                                         ).then_inc(o_normed, 1)

            def conv(c):
                dve.wait_ge(z_set, c + 1)
                if c > 0:
                    dve.wait_ge(yb_set, c)
                for m in range(3):
                    tap = row_of["conv_w"] + 2 * m + c
                    z = zp[:, c, m:m + ZW - 2]
                    if m == 0:
                        dve.tensor_scalar(cacc, z, cols[:, tap:tap + 1], None, ALU.mult).then_inc(conv_acc, 1)
                    else:
                        dve.wait_ge(conv_acc, 3 * c + m)
                        dve.scalar_tensor_tensor(cacc, z, cols[:, tap:tap + 1], cacc, ALU.mult, ALU.add
                                                 ).then_inc(conv_acc, 1)

            def y_part(k):
                dve.wait_ge(y_hi, k + 1)
                dve.tensor_tensor(xl[:, k, :], y_of(k), xh[:, k, :].bitcast(F32), ALU.subtract
                                  ).then_inc(y_lo, 1)

            scale_r(0)
            o_invert(0)
            split_lo(u_r[2])
            o_norm(0)
            conv(0)
            o_invert(1)
            scale_r(1)
            split_lo(u_r[3])
            o_norm(1)
            o_invert(2)
            o_norm(2)
            conv(1)
            scale_r(2)
            split_lo(u_wo[0])
            o_invert(3)
            o_norm(3)
            scale_r(3)
            y_part(0)
            y_part(1)
            split_lo(u_wo[1])
            for k in range(2, KT):
                y_part(k)
            dve.wait_ge(reloaded, 16)
            for j in range(KT):
                if 0 < j < KT - 1:
                    split_lo(u_wo[j + 1])
                src = result(g_wo[j])
                dve.tensor_tensor(blocks(x[:, j, :]), src, blocks(x[:, j, :]), ALU.add
                                  ).then_inc(free[g_wo[j][0]], 1)
            split_lo(ffn2.unit)
            for j in range(KT):
                x_lo(2, j)
            pair = ffn(ffn2, PAIRS, 2)
            pair(0, first=True)
            dve.wait_ge(wp_hi, 1)
            dve.tensor_tensor(wpl[:], wpst[:], wph[:].bitcast(F32), ALU.subtract).then_inc(wp_lo, 1)
            with dve.Fori(1, PAIRS - 1) as i:
                pair(i)
            pair(PAIRS - 1, last=True)

            for c in range(2):
                dve.wait_ge(p_hi, c + 1)
                dve.tensor_tensor(hl[:, c, :], p_t[:, c, :], hh[:, c, :].bitcast(F32), ALU.subtract
                                  ).then_inc(p_lo, 1)
            for j in range(KT):
                if j < KT - 1:
                    split_lo(u_ple[j + 1])
                if j == 0:
                    finish_norm(3)
                    dve.wait_ge(r_set, 8)
                src = result(g_gate[j])
                if j > 0:
                    dve.wait_ge(gate_sig, j)
                dve.tensor_tensor(blocks(tg[:]), src, blocks(r[:]), ALU.mult).then_inc(free[SET_A], 1)
                src = result(g_proj[j])
                dve.wait_ge(gate_sig, j + 1)
                if j > 0:
                    dve.wait_ge(x_added, j)
                dve.tensor_tensor(blocks(h32[:]), src, blocks(sg[:]), ALU.mult).then_inc(ple_set, 1)

            dve.wait_ge(gf_in, 16)
            for t in range(NTILE + 1):
                rs = slice(0, P) if t < NTILE else slice(P - dec, P)
                dve.wait_ge(fin_root, t + 1)
                dve.reciprocal(ricol[rs, t:t + 1], rcol[rs, 1:2]).then_inc(fin_inv, 1)
                dve.wait_ge(fin_inv, t + 1)
                if t > 1:
                    dve.wait_ge(outs[t % 2], 16 * (t // 2))
                dve.scalar_tensor_tensor(y_out(t)[rs].rearrange("p (b n) -> p b n", b=2), fin_ps(t)[rs],
                                         ricol[rs, t:t + 1], g_final[rs].rearrange("p (b n) -> p b n", b=2),
                                         ALU.mult, ALU.mult).then_inc(fin_set, 1)

        @block.tensor
        def _(pe):
            def mm(out, w_, x_, start, stop, skip=False):
                return pe.matmul(out, w_, x_, start=start, stop=stop)

            def wait_free(s, use, i=0):
                if isinstance(i, int) and i == 0:
                    if use > 0:
                        pe.wait_ge(free[s], released[s][use - 1])
                else:
                    step = RELEASES[s]
                    pe.wait_ge(free[s], at_step(released[s][use - 1 + STEP] - step, i, step))

            def three_passes(out, w_hi_, w_lo_, x_hi_, x_lo_, blks, start, stop):
                for w_, x_ in ((w_hi_, x_hi_), (w_hi_, x_lo_), (w_lo_, x_hi_)):
                    for blk in blks:
                        last = pe.matmul(out(blk), w_, x_[:, blk * TB:blk * TB + TB],
                                         start=start and w_ is w_hi_ and x_ is x_hi_,
                                         stop=stop and w_ is w_lo_)
                return last

            def project(n, s, i=0, ready=None, hooks={}, by_block=None):
                pe.wait_ge(w_lo, at_step(n + 1, i))
                b = n % 2

                def tile(k, blks):
                    return three_passes(lambda blk: ps[:, SETS[s] + blk, 0:TB], wh[b][:, k, :],
                                        wl[b][:, k, :], xh[:, k, :], xl[:, k, :], blks, k == 0, k == KT - 1)

                if by_block is not None:
                    for blk in range(NB):
                        for k in range(KT):
                            last = tile(k, (blk,))
                        last.then_inc(up_block if blk < NB - 1 else full[s], 1)
                    return
                for k in range(KT):
                    if ready is not None:
                        pe.wait_ge(ready[0], ready[1] + k + 1)
                    last = tile(k, range(NB))
                    if k == KT - 1:
                        last.then_inc(full[s], 1)
                    if k in hooks:
                        hooks[k]()

            def sums(column_sums, rows_sem, rows_val, signal):
                pe.wait_ge(rows_sem, rows_val)
                for t in range(NTILE + 1):
                    w = P if t < NTILE else dec
                    last = pe.matmul(ps[0:w, 6, t:t + 1], column_sums[:, t * P:t * P + w], ones[:, 0:1],
                                     start=True, stop=True)
                last.then_inc(signal, 1)

            def spread(dg, signal):
                for m in range(2):
                    last = pe.matmul(ps[:, 6 + m, :], ones[:], dg[:, m * 512:m * 512 + 512],
                                     start=True, stop=True)
                last.then_inc(signal, 1)

            def spread_sample(dg, signal):
                pe.matmul(ps[:, 6, 0:dec], ones[0:dec, :], dg[0:dec, seq:T], start=True, stop=True
                          ).then_inc(signal, 1)

            def norm_sums(norm):
                sums(acc, sq_added, (KT - 1) * (norm + 1), rs_cols)

            def norm_spread(norm):
                pe.wait_ge(diag_set, norm + 1)
                spread(diag, r_full)

            def norm_spread_sample(norm):
                pe.wait_ge(r_set, 2 * norm + 1)
                spread_sample(diag, r_full)

            def ffn(f, before, norm, last_hooks={}):
                def pair(i, first=False, last=False):
                    k = before + i
                    nh = (1 + NB) * k
                    n = f.unit
                    wait_free(SET_A, f.a, i)
                    project(n, SET_A, i, (xg_lo, KT * norm) if first else None,
                            {3: lambda: norm_sums(norm)} if first else last_hooks if last else {})
                    wait_free(SET_B, f.b, i)
                    project(n + 1, SET_B, i, None,
                            {0: lambda: norm_spread(norm), 4: lambda: norm_spread_sample(norm)}
                            if first else {})
                    wait_free(SET_A, f.a + 1, i)
                    project(n + 2, SET_A, i)
                    pe.wait_ge(h_set, nh + 1)
                    project(n + 3, SET_B, i, by_block=True)
                    for j in range(KT):
                        s = j % 2
                        if j % 4 == 0:
                            pe.wait_ge(w_lo, at_step(n + 5 + j // 4, i))
                        if j == 1:
                            pe.wait_ge(h_set, nh + 1 + NB)
                        else:
                            wait_free(s, (f.a, f.b)[s] + 2 + j // 2, i)
                        b = (n + 4 + j // 4) % 2

                        def down(q, blks):
                            m = q * 4 + j % 4
                            return three_passes(lambda blk: ps[:, SETS[s] + blk, 0:TB], wh[b][:, m, :],
                                                wl[b][:, m, :], hh[:, q, :], hl[:, q, :], blks,
                                                q == 0, q == 1)
                        if j == 0:
                            pe.wait_ge(h_lo, nh + 1)
                        last_mm = down(0, range(NB))
                        if j == 0:
                            for blk in range(NB):
                                pe.wait_ge(h_lo, nh + 2 + blk)
                                last_mm = down(1, (blk,))
                        else:
                            last_mm = down(1, range(NB))
                        last_mm.then_inc(full[s], 1)
                return pair

            pe.wait_ge(ones_set, 4)
            pe.wait_ge(small_in, 16 * len(ROWS))
            pe.transpose(ps[:, 7, 0:n_rows], rows[0:n_rows, :], ident[0:n_rows, 0:n_rows]).then_inc(rows_t, 1)
            for t in range(NTILE + 1):
                if t % 4 == 0:
                    pe.wait_ge(x_in[t // 4], 16)
                if t > 1:
                    pe.wait_ge(xt_done, t - 1)
                w = P if t < NTILE else dec
                src = xin[:, t, :] if t < NTILE else xin_s[0:dec, :]
                for j in range(KT):
                    last = pe.transpose(ps[:, 2 * (t % 2) + j // 4, j % 4 * P:j % 4 * P + w],
                                        src[:, j * P:j * P + P], ident[0:w, 0:w])
                last.then_inc(xt_full, 1)
            pe.wait_ge(xt_done, NTILE + 1)
            pe.wait_ge(cols_set, 1)
            pair = ffn(ffn1, 0, 0)
            pair(0, first=True)
            with pe.Fori(1, PAIRS - 1) as i:
                pair(i)
            pair(PAIRS - 1, last=True)

            wait_free(*g_gl)
            project(u_gl, SET_A, 0, (xg_lo, KT), {3: lambda: norm_sums(1)})
            wait_free(*g_va[0])
            project(u_va[0], SET_B, hooks={0: lambda: norm_spread(1), 4: lambda: norm_spread_sample(1)})
            wait_free(*g_va[1])
            project(u_va[1], SET_A)
            pe.wait_ge(ws_masked, 1)
            pe.wait_ge(r_set, 4)
            for h in range(heads):
                last = pe.transpose(ps[:, 6, h * P:h * P + P], ws_in[:, h, :], ident[:])
            last.then_inc(ws_full, 1)
            pe.wait_ge(mix_in, 16 * 7)
            s, use = g_gl
            pe.wait_ge(free[s], released[s][use])
            for c in range(NPAIR):
                s, use = g_z[c]
                wait_free(s, use)
                for blk in range(NB):
                    last = pe.matmul(ps[:, SETS[s] + blk, 0:TB], w2[0:rank, c * P:c * P + P],
                                     gl[:, blk * TB:blk * TB + TB], start=True, stop=True)
                last.then_inc(full[s], 1)
            for u, (s, use) in zip(u_qkv, g_qkv):
                wait_free(s, use)
                project(u, s)
            pe.wait_ge(ws_set, 1)

            def mixers(p, e, w=P):
                t = 2 * p + e
                first = isinstance(t, int) and t == 0
                sample = w < P
                nblk = 1 if sample else 2
                pe.wait_ge(st_a_set, t + 1)
                if first:
                    pe.wait_ge(free[SET_B], released[SET_B][g_qkv[6][1]])
                else:
                    pe.wait_ge(gm_set, t)
                    pe.wait_ge(va_n_set, t)
                for h in range(heads):
                    pe.transpose(ps[:, 3, h * P:h * P + P], st_a[:, V_ + h, :], ident[:])
                for c in range(2):
                    pe.transpose(ps[:, 4, c * P:c * P + P], st_a[:, KE + c, :], ident[:])
                for c in range(2):
                    last = pe.transpose(ps[:, 4, 2 * P + c * P:3 * P + c * P], st_a[:, VA + c, :], ident[:])
                last.then_inc(tile_t, 1)
                pe.wait_ge(st_q_set, t + 1)
                if not first:
                    pe.wait_ge(a_bounded, t)
                for h in range(heads):
                    last = pe.matmul(ps[0:w, 5, h * P:h * P + w], st_a[:, K_ + h // 2, 0:w],
                                     st_q[:, h, 0:w], start=True, stop=True)
                last.then_inc(a_full, 1)

                n = u_big[0] + e
                b = n % 2
                pe.wait_ge(w_lo, n + 1 + 2 * p)
                pe.wait_ge(free[SET_A], released[SET_A][g_big[0][1]] - 1 + t)

                def beside(ks):
                    for k in ks:
                        last = three_passes(lambda blk: ps[:, blk, 0:TB], wh[b][:, k, :], wl[b][:, k, :],
                                            xh[:, k, :], xl[:, k, :], range(NB), k == 0, k == KT - 1)
                        if k == KT - 1:
                            last.then_inc(full[SET_A], 1)

                beside((0, 1, 2))
                pe.wait_ge(ke_n_set, t + 1)
                pe.wait_ge(v_n_set, t + 1)
                if not first:
                    pe.wait_ge(s0_set, t)
                for m in range(nblk):
                    for h in range(heads):
                        c, q = h // 2, h % 2
                        last = pe.matmul(ps[64 * q:64 * q + 64, 7, (2 * m + c) * P:(2 * m + c + 1) * P],
                                         ke_n[0:w, m, c * P + 64 * q:c * P + 64 * q + 64],
                                         v_n[0:w, h * P:h * P + P], start=True, stop=True)
                last.then_inc(ds_full, 1)
                pe.wait_ge(va_n_set, t + 1)
                for h in range(heads):
                    c, q = h // 2, h % 2
                    last = pe.matmul(ps[64 * q:64 * q + 64, 3, c * P:c * P + w],
                                     va_n[0:w, h * 64:h * 64 + 64], ws_t[0:w, h, 0:w],
                                     start=True, stop=True)
                last.then_inc(gm_full, 1)
                beside((3, 4, 5))
                pe.wait_ge(a_masked, t + 1)
                pe.wait_ge(s1_set, t + (0 if sample else 1))
                if not first:
                    pe.wait_ge(o_set, t)
                for h in range(heads):
                    pe.matmul(ps[:, 6, h * P:h * P + w], v_n[0:w, h * P:h * P + P], a_t[0:w, h, 0:w],
                              start=True, stop=False)
                    for m in range(nblk):
                        state = s_in if sample else (s0, s1)[m]
                        bw = w // nblk
                        last = pe.matmul(ps[:, 6, h * P + m * bw:h * P + m * bw + bw], state[:, h // 2, :],
                                         st_q[:, h, m * bw:m * bw + bw], start=False, stop=m == nblk - 1)
                last.then_inc(o_full, 1)
                beside((6, 7))

            over_token_tiles(pe, mixers)

            def o_sums(h):
                if h == 0:
                    pe.wait_ge(o_set, NTILE + 1)
                else:
                    pe.wait_ge(o_normed, 2 * h)
                sums(osq, osq_set, h + 1, os_cols)

            def o_spread(h):
                pe.wait_ge(odiag_set, h + 1)
                spread(diag_o, or_full)

            def o_spread_sample(h):
                pe.wait_ge(o_normed, 2 * h + 1)
                spread_sample(diag_o, or_full)

            r_hooks = [{0: lambda: o_sums(0), 3: lambda: o_spread(0), 5: lambda: o_spread_sample(0),
                        6: lambda: o_sums(1)},
                       {0: lambda: o_spread(1), 2: lambda: o_spread_sample(1), 3: lambda: o_sums(2),
                        5: lambda: o_spread(2), 6: lambda: o_spread_sample(2)},
                       {0: lambda: o_sums(3), 2: lambda: o_spread(3), 4: lambda: o_spread_sample(3)}]
            for done_with_bank in (gm_set, va_n_set, a_bounded):
                pe.wait_ge(done_with_bank, NTILE + 1)
            for h in range(1, heads):
                wait_free(*g_r[h])
                project(u_r[h], g_r[h][0], hooks=r_hooks[h - 1])
            for j in range(KT):
                wait_free(*g_wo[j])
                project(u_wo[j], g_wo[j][0], 0, (y_lo, 0) if j == 0 else None)

            def p_round(g):
                if g == 0:
                    pe.wait_ge(p_in, 48)
                else:
                    pe.wait_ge(p_copied, g)
                for t in range(4 * g, min(4 * g + 4, NTILE + 1)):
                    w = P if t < NTILE else dec
                    for c in range(2):
                        last = pe.transpose(ps[:, 6 + c, t % 4 * P:t % 4 * P + w],
                                            pnat[0:w, t, c * P:c * P + P], ident[0:w, 0:w])
                last.then_inc(p_full, 1)

            pair = ffn(ffn2, PAIRS, 2, {2 * g + 1: (lambda g=g: p_round(g)) for g in range(NROUND)})
            pair(0, first=True)
            with pe.Fori(1, PAIRS - 1) as i:
                pair(i)
            pair(PAIRS - 1, last=True)

            for j in range(KT):
                wait_free(*g_gate[j])
                project(u_ple[j], SET_A, 0, (xg_lo, KT * 3) if j == 0 else None,
                        {2: lambda: norm_sums(3), 5: lambda: norm_spread(3),
                         6: lambda: norm_spread_sample(3)} if j == 0 else {})
                if j == 0:
                    wait_free(*g_proj[0])
                    pe.wait_ge(p_lo, 2)
                    pe.wait_ge(wp_lo, 1)
                else:
                    pe.wait_ge(ple_set, j)
                for c in range(2):
                    last = three_passes(lambda blk: ps[:, SETS[SET_B] + blk, 0:TB],
                                        wph[:, c, j * P:j * P + P], wpl[:, c, j * P:j * P + P],
                                        hh[:, c, :], hl[:, c, :], range(NB), c == 0, c == 1)
                last.then_inc(full[SET_B], 1)

            pe.wait_ge(x_added, KT)
            pe.wait_ge(ple_set, KT)
            for t in range(NTILE + 1):
                if t > 1:
                    pe.wait_ge(fin_set, t - 1)
                t0 = t * P if t < NTILE else T - P
                for j in range(KT):
                    last = pe.transpose(ps[:, 2 * (t % 2) + j // 4, j % 4 * P:j % 4 * P + P],
                                        x[:, j, t0:t0 + P], ident[:])
                last.then_inc(fin_full, 1)

    return nc


_INS = ["x_prompt", "x_sample", "p_prompt", "p_sample", "state_conv", "state_gla", "norm_ffn1",
        "w_ffn1_gate", "w_ffn1_up", "w_ffn1_down", "norm_mix", "w_in", "w_s", "b_s", "conv_w", "w_gate2",
        "b_gate2", "gla_norm", "w_o", "norm_ffn2", "w_ffn2_gate", "w_ffn2_up", "w_ffn2_down", "norm_ple",
        "w_ple_gate", "w_ple_proj", "final_norm"]


def kernel(**inputs):
    import numpy as _np
    import concourse.bacc as _bacc
    from concourse.bass_utils import run_bass_kernel_spmd as _run

    nc = _bacc.Bacc("TRN2", target_bir_lowering=False, num_devices=1)
    arrays, ins = {}, {}
    for name in _INS:
        v = _np.ascontiguousarray(inputs[name])
        arrays[f"in_{name}"] = v
        ins[name] = nc.dram_tensor(f"in_{name}", v.shape, mybir.dt.from_np(v.dtype), kind="ExternalInput").ap()
    depth, _, seq, _ = inputs["p_prompt"].shape
    d = inputs["x_prompt"].shape[2]
    _, batch, dec, _ = inputs["p_sample"].shape
    heads, dk, dv = inputs["state_gla"].shape[2:]
    taps, d_b = inputs["conv_w"].shape[1:]
    d_a = d // 4
    shapes = [(1, seq, d), (batch, dec, d), (depth, 1, taps - 1, d_b), (depth, 1, heads, dk, dv),
              (depth, batch, taps - 1, d_b), (depth, batch, heads, dk, dv), (depth, batch, dec, d_a)]
    outs = [nc.dram_tensor(f"out_{i}", s, F32, kind="ExternalOutput").ap() for i, s in enumerate(shapes)]
    hybrid_trunk(nc, ins, outs)
    got = _run(nc, [arrays], core_ids=[0])
    return tuple(got.results[0][f"out_{i}"] for i in range(len(shapes)))
```

```python
from contextlib import ExitStack

import concourse.bass as bass
from concourse import mybir

P = 128
F32 = mybir.dt.float32
F32R = mybir.dt.float32r
ALU = mybir.AluOpType
ACT = mybir.ActivationFunctionType


def hybrid_trunk(nc, a, o):
    (y_prompt, y_sample, conv_prompt, gla_prompt, conv_sample, gla_sample, v_sample) = o
    depth, batch, seq, d_ple = a["p_prompt"].shape
    _, dec_batch, dec, d = a["x_sample"].shape[0:1] + a["x_sample"].shape[0:1] + a["x_sample"].shape[1:]
    assert depth == 1 and batch == 1 and dec_batch == 1
    ff = a["w_ffn1_gate"].shape[2]
    T = seq + dec
    KT = d // P
    FT = ff // P
    NB = 3
    TB = T // NB
    assert TB * NB == T and TB <= 512 and FT % 2 == 0
    NTILE = seq // P
    heads, dk, dv = a["state_gla"].shape[2:]
    L = 64
    NPAIR = heads // 2
    d_a = a["w_s"].shape[1] * 64
    rank = a["w_gate2"].shape[1]
    TAU = 16.0
    EPS = 1e-6
    D_C = heads * dv
    assert dec <= L and 2 * dk == P and dv == P and d_a == 2 * P

    COL_U, COL_VA, COL_B, COL_C, COL_X, COL_Q, COL_K, COL_V, COL_R = 0, 2, 4, 6, 8, 10, 12, 14, 18
    COL_GL = 22 * P
    GLW = 2 * rank
    GL_ROWS = 3 * GLW

    PAIRS = FT // 2
    STEP = 6
    SET_A, SET_B = 0, 1
    uses = [0, 0]
    released = [[], []]
    done = []

    def take(s, counted=True):
        uses[s] += 1
        released[s].append((released[s] or [0])[-1] + counted)
        return s, uses[s] - 1

    def take_unit(use):
        done.append((use[0], use[1] + 1))
        return len(done) - 1

    class Ffn:

        def __init__(self):
            self.unit, self.a, self.b = len(done), uses[SET_A], uses[SET_B]
            for _ in range(PAIRS):
                for _ in range(2):
                    take_unit(take(SET_A))
                    take_unit(take(SET_B, counted=False))
                for _ in range(2):
                    tiles = [take((SET_A, SET_B)[j % 2]) for j in range(4)]
                    take_unit(tiles[3])

        def down(self, j, pair=PAIRS - 1):
            return j % 2, (self.a, self.b)[j % 2] + STEP * pair + 2 + j // 2

    ffn1 = Ffn()
    g_gl = take(SET_A)
    u_gl = take_unit(g_gl)
    g_va = [take(SET_B), take(SET_A)]
    u_va = [take_unit(g) for g in g_va]
    g_z = [take(SET_B), take(SET_A)]
    g_qkv = [take((SET_B, SET_A)[i % 2]) for i in range(8)]
    u_qkv = [take_unit(g) for g in g_qkv]
    g_big = [take(SET_A) for _ in range(NTILE + 1)]
    u_big = [take_unit(g) for g in g_big]
    g_r = g_big[NTILE:] + [take((SET_B, SET_A)[i % 2]) for i in range(3)]
    u_r = u_big[NTILE:] + [take_unit(g) for g in g_r[1:]]
    g_wo = [take((SET_A, SET_B)[j % 2]) for j in range(KT)]
    u_wo = [take_unit(g) for g in g_wo]
    ffn2 = Ffn()
    g_gate = [take(SET_A) for _ in range(KT)]
    g_proj = [take(SET_B, counted=False) for _ in range(KT)]
    FIN_TILES = [range(0, TB // P), range(TB // P, 2 * TB // P), range(2 * TB // P, NTILE + 1)]
    u_ple = [take_unit(g) for g in g_gate]

    TILE_ENDS = [-(-(b + 1) * TB // P) for b in range(NB)]
    BY_ACT = [1, 3, 5, 6, 7]

    def xg_before(norm):
        return KT * (norm + NB - 1) if norm > 0 else 0

    RELEASES = (STEP, STEP - 2)
    NROUND = 3
    N_STATE_OUT = 9
    N_MIX_IN = GL_ROWS // rank + heads + 2

    def at_step(value, i, add=STEP):
        return value + add * i

    def used_up(n, i=0):
        if isinstance(i, int):
            n, i = n + STEP * i, 0
            return done[n - 2]
        s, count = done[n - 2 + STEP]
        return s, count - STEP + STEP * i

    ctx = ExitStack()
    with ctx:
        base = (nc.sbuf_base + 63) // 64 * 64
        top = [base]

        def at(name, shape, dt=F32, offset=None):
            n = 4
            for s in shape[1:]:
                n *= s
            if offset is None:
                offset = top[0]
                top[0] += (n + 31) // 32 * 32
            return nc.alloc_sbuf_tensor_at(name, shape, dt, offset=offset)

        x = at("x", [P, KT, T])
        late = x
        xh = at("xh", [P, KT, T], F32R)
        xl = at("xl", [P, KT, T], F32R)
        wst = [at(f"wst{b}", [P, KT, P]) for b in range(2)]
        wh = [at(f"wh{b}", [P, KT, P], F32R) for b in range(2)]
        wl = [at(f"wl{b}", [P, KT, P], F32R) for b in range(2)]
        r = at("r", [P, T])
        acc = at("acc", [P, T])
        ident = at("ident", [P, P])
        ones = at("ones", [P, P])
        rows = at("rows", [P, P])
        cols = at("cols", [P, 48])
        eps = at("eps", [P, 1])
        ss = at("ss", [P, NTILE + 1])
        rcol = at("rcol", [P, heads * (NTILE + 1)])
        ricol = at("ricol", [P, heads * (NTILE + 1)])
        phase = top[0]
        hh = at("hh", [P, 2, T], F32R)
        hl = at("hl", [P, 2, T], F32R)
        tg = at("tg", [P, T])
        sg = at("sg", [P, T])
        sr = at("sr", [P, T])
        h32 = at("h32", [P, T])
        sq = at("sq", [P, 2, T])
        ple = top[0]
        pnat = at("pnat", [P, NTILE + 1, d_ple])
        p_t = at("p_t", [P, 2, T])
        wpst = at("wpst", [P, 2, d], offset=p_t.manual_sbuf_range[0])
        wph = at("wph", [P, 2, d], F32R)
        wpl = at("wpl", [P, 2, d], F32R)
        ffn_end = top[0]
        xin = at("xin", [P, NTILE, d], offset=ple)
        ffn_end = max(ffn_end, ple + NTILE * d * 4)
        xin_s = tg[:, 0:d]
        top[0] = phase
        mix = at("mix", [P, 12, T])
        K_, KE, V_, VA, Q_ = 0, 2, 4, 8, 10
        st_a = at("st_a", [P, 10, P])
        st_q = at("st_q", [P, heads, P])
        ke_n = at("ke_n", [P, 2, 2 * P])
        v_n = at("v_n", [P, D_C])
        a_t = at("a_t", [P, heads, P])
        va_n = at("va_n", [P, d_a])
        ws_t = at("ws_t", [P, heads, P])
        bias = at("bias", [P, NPAIR, P])
        s0 = at("s0", [P, NPAIR, P])
        s1 = at("s1", [P, NPAIR, P])
        s_in = at("s_in", [P, NPAIR, P])
        decay = at("decay", [P, NPAIR, 2 * NTILE + 1])
        w2 = at("w2", [P, 2 * P])
        ln = at("ln", [P, 16])
        keep_hi = at("keep_hi", [P, P])
        keep_lo = at("keep_lo", [P, P])
        top[0] = max(top[0], ffn_end)
        assert top[0] <= nc.sbuf_usable_end, (top[0], nc.sbuf_usable_end)
        gl = mix[0:GL_ROWS, V_, :]
        gl_parts = at("gl_parts", [P, T], F32R, offset=st_a.manual_sbuf_range[0])[0:GL_ROWS]
        w2_parts = at("w2_parts", [P, 2 * P], F32R, offset=v_n.manual_sbuf_range[0])[0:GL_ROWS]
        ws_in = st_q
        reset = acc
        flat = mix[:].rearrange("p a b -> p (a b)")
        ZW = T + 4
        zp = flat[:, 0:2 * ZW].rearrange("p (c t) -> p c t", c=2)
        cacc = flat[:, 2 * ZW:3 * ZW - 2]
        r_gate = at("r_gate", [P, T], offset=ke_n.manual_sbuf_range[0])
        osq = acc
        assert ke_n.manual_sbuf_range[0] + T * 4 <= a_t.manual_sbuf_range[1] and 3 * ZW <= 4 * T

        ps = ctx.enter_context(nc.psum_tensor("ps", [P, 8, 512], F32))
        SETS = (0, 3)
        x_dram = nc.dram_tensor("x_spill", [P, KT, T], F32).ap()

        def sem(name):
            return ctx.enter_context(nc.semaphore(name))

        w_landed = [sem(f"w_landed{b}") for b in range(2)]
        w_hi = sem("w_hi")
        w_lo = sem("w_lo")
        w_lo_pool = sem("w_lo_pool")
        full = [sem("full_a"), sem("full_b")]
        free = [sem("free_a"), sem("free_b")]
        up_block = sem("up_block")
        ones_set = sem("ones_set")
        mask_set = sem("mask_set")
        small_in = sem("small_in")
        gain_in = sem("gain_in")
        x_in = [sem(f"x_in{i}") for i in range(NTILE + 1)]
        rows_t = sem("rows_t")
        cols_set = sem("cols_set")
        xt_full = sem("xt_full")
        xt_dve = sem("xt_dve")
        xt_act = sem("xt_act")
        x_sq = sem("x_sq")
        xh_used = sem("xh_used")
        xg_hi = sem("xg_hi")
        xg_lo = sem("xg_lo")
        sq_set = sem("sq_set")
        sq_added = sem("sq_added")
        rs_cols = sem("rs_cols")
        rms_set = sem("rms_set")
        inv_set = sem("inv_set")
        r_full = sem("r_full")
        r_set = sem("r_set")
        g_silu = sem("g_silu")
        g_silu_r = sem("g_silu_r")
        h_set = sem("h_set")
        h_hi = sem("h_hi")
        h_lo = sem("h_lo")
        spilled = sem("spilled")
        reloaded = sem("reloaded")
        ws_landed = sem("ws_landed")
        mix_in = sem("mix_in")
        ws_masked = sem("ws_masked")
        ws_full = sem("ws_full")
        ws_set = sem("ws_set")
        gl_set = sem("gl_set")
        gl_low = sem("gl_low")
        w2_set = sem("w2_set")
        w2_low = sem("w2_low")
        z_abs = sem("z_abs")
        z_exp = sem("z_exp")
        z_log = sem("z_log")
        ls_set = sem("ls_set")
        reset_set = sem("reset_set")
        g_cum = sem("g_cum")
        e_pos = sem("e_pos")
        e_neg = sem("e_neg")
        decay_set = sem("decay_set")
        e_r = sem("e_r")
        ke_set = sem("ke_set")
        zeroed = sem("zeroed")
        st_a_set = sem("st_a_set")
        st_q_set = sem("st_q_set")
        tile_t = sem("tile_t")
        a_full = sem("a_full")
        ds_full = sem("ds_full")
        gm_full = sem("gm_full")
        o_full = sem("o_full")
        v_n_set = sem("v_n_set")
        a_bounded = sem("a_bounded")
        a_masked = sem("a_masked")
        ke_n_set = sem("ke_n_set")
        ln_stat = sem("ln_stat")
        ln_mean = sem("ln_mean")
        ln_root = sem("ln_root")
        ln_inv = sem("ln_inv")
        va_n_set = sem("va_n_set")
        s1_set = sem("s1_set")
        s0_set = sem("s0_set")
        gm_set = sem("gm_set")
        o_set = sem("o_set")
        z_set = sem("z_set")
        conv_begun = sem("conv_begun")
        conv_acc = sem("conv_acc")
        ya_set = sem("ya_set")
        yb_set = sem("yb_set")
        yc_set = sem("yc_set")
        yc_last = sem("yc_last")
        osq_set = sem("osq_set")
        os_cols = sem("os_cols")
        orms_set = sem("orms_set")
        oinv_set = sem("oinv_set")
        or_samples = sem("or_samples")
        or_full = sem("or_full")
        o_normed = sem("o_normed")
        r_silu = sem("r_silu")
        y_hi = sem("y_hi")
        y_lo = sem("y_lo")
        p_in = sem("p_in")
        p_full = sem("p_full")
        p_copied = sem("p_copied")
        p_hi = sem("p_hi")
        p_lo = sem("p_lo")
        wp_hi = sem("wp_hi")
        wp_lo = sem("wp_lo")
        gate_sig = sem("gate_sig")
        ple_set = sem("ple_set")
        x_added = sem("x_added")
        gf_in = sem("gf_in")
        last_gate = sem("last_gate")
        last_proj = sem("last_proj")
        last_scaled = sem("last_scaled")
        last_sig = sem("last_sig")
        last_ple = sem("last_ple")
        last_added = sem("last_added")
        fin_full = sem("fin_full")
        fin_sq = sem("fin_sq")
        fin_root = sem("fin_root")
        fin_inv = sem("fin_inv")
        fin_set = sem("fin_set")
        outs = [sem(f"outs{i}") for i in range(4)]
        state_out = sem("state_out")

        block = ctx.enter_context(nc.Block())

        def banks(s):
            return ps[:, SETS[s]:SETS[s] + NB, 0:TB]

        def over_token_tiles(eng, body):
            body(0, 0)
            body(0, 1)
            with eng.Fori(1, NTILE // 2) as p:
                body(p, 0)
                body(p, 1)
            body(NTILE // 2, 0, dec)

        r_sample = ps[:, SETS[SET_A], TB:TB + dec]

        def or_sample(h):
            return ps[:, SETS[g_r[1][0]], TB + h * dec:TB + (h + 1) * dec]

        def y_of(k):
            return mix[:, (VA, VA + 1, Q_, Q_ + 1, V_, V_ + 1, V_ + 2, V_ + 3)[k], :]

        g_final = pnat[:].rearrange("p a b -> p (a b)")[:, 0:d]

        def y_out(t):
            return (sq if t % 4 < 2 else p_t)[:, t % 2, 0:d]

        X_BANKS = [(3, 5, 1)[t % 3] if t < TILE_ENDS[1] else (3, 5)[t % 2] for t in range(NTILE)] + [7]

        def x_ps(t):
            b = X_BANKS[t]
            if t == NTILE:
                return ps[:, b, 0:KT * dec].rearrange("p (j n) -> p j n", n=dec)
            return ps[:, b:b + 2, :].rearrange("p b (j n) -> p (b j) n", n=P)

        def rows_of(t):
            return slice(t * P, min(t * P + P, T))

        def rank_parts(b, m):
            return wh[b][:, :, 0:GL_ROWS].rearrange("p k (c m r) -> p k c m r", c=3, m=2)[:, :, :, m, :]

        def rank_columns(b):
            return wst[b][:, :, 0:rank].unsqueeze(2).broadcast_to([P, KT, 3, rank])

        def wait_copied(eng, n):
            by_act = sum(t < n for t in BY_ACT)
            if n > by_act:
                eng.wait_ge(xt_dve, n - by_act)
            if by_act:
                eng.wait_ge(xt_act, by_act)

        def fin_bank(t):
            return (6, 0, 2, 6, 0, 4, 2, 6, 0)[t]

        def fin_ps(t):
            return ps[:, fin_bank(t):fin_bank(t) + 2, :]

        def fin_row(t):
            return slice(0, P) if t < NTILE else slice(P - dec, P)

        def blocks(t):
            return t.rearrange("p (b n) -> p b n", b=NB)

        ROWS = [("norm_ffn1", KT), ("norm_mix", KT), ("norm_ffn2", KT), ("norm_ple", KT),
                ("gla_norm", heads), ("conv_w", 6), ("state_conv", 4), ("b_gate2", 2)]
        row_of, n_rows = {}, 0
        for name, n in ROWS:
            row_of[name] = n_rows
            n_rows += n
        assert n_rows <= 48
        GAIN = [row_of[n] for n in ("norm_ffn1", "norm_mix", "norm_ffn2", "norm_ple")]

        def gain(norm, j):
            return cols[:, GAIN[norm] + j:GAIN[norm] + j + 1]

        def wait_used(eng, n, i=0):
            if isinstance(i, int) and n + STEP * i < 2:
                return
            s, count = used_up(n, i)
            eng.wait_ge(full[s], count)

        @block.sync
        def _(sp):
            def load(n, src, i=0, dst=None):
                b = n % 2
                if not (isinstance(i, int) and n + STEP * i < 2):
                    sp.wait_ge(w_lo, at_step(n - 1, i))
                sp.dma_start(wst[b][:] if dst is None else dst, src).then_inc(w_landed[b], 16)

            def column_tile(w, cs):
                return w[0, :, cs].rearrange("(k p) n -> p k n", p=P)

            def load_pair(f, wg, wu, wd, i, loaded=0):
                for q in range(loaded, 2):
                    cs = bass.ds(i * 2 * P + q * P, P)
                    load(f.unit + 2 * q, column_tile(wg, cs), i)
                    load(f.unit + 2 * q + 1, column_tile(wu, cs), i)
                for half in range(2):
                    n = f.unit + 4 + half
                    src = wd[0, bass.ds(i * 2 * P, 2 * P), half * 4 * P:(half + 1) * 4 * P]
                    load(n, src.rearrange("(k p) n -> p k n", p=P), i,
                         wst[n % 2][:].rearrange("p (k q) n -> p k (q n)", k=2))

            ffn_w1 = (a["w_ffn1_gate"], a["w_ffn1_up"], a["w_ffn1_down"])
            ffn_w2 = (a["w_ffn2_gate"], a["w_ffn2_up"], a["w_ffn2_down"])

            def load_row(name, n, signal):
                v = a[name][0] if name != "state_conv" else a[name][0, 0]
                v = v.rearrange("w (c p) -> (w c) p", p=P) if len(v.shape) == 2 else \
                    v.rearrange("(c p) -> c p", p=P)
                sp.dma_start(rows[row_of[name]:row_of[name] + n, :], v).then_inc(signal, 16)

            def load_x(t):
                if t < NTILE:
                    sp.dma_start(xin[:, t, :], a["x_prompt"][0, t * P:t * P + P, :]).then_inc(x_in[t], 16)
                else:
                    sp.dma_start(xin_s[0:dec, :], a["x_sample"][0]).then_inc(x_in[t], 16)

            load_x(0)
            load_row(*ROWS[0], gain_in)
            for t in range(1, TILE_ENDS[0]):
                load_x(t)
            load(ffn1.unit, column_tile(ffn_w1[0], slice(0, P)))
            for t in range(TILE_ENDS[0], TILE_ENDS[1]):
                load_x(t)
            for name, n in ROWS[1:]:
                load_row(name, n, small_in)
            for t in range(TILE_ENDS[1], NTILE + 1):
                load_x(t)
            load(ffn1.unit + 1, column_tile(ffn_w1[1], slice(0, P)))
            sp.wait_ge(w_lo_pool, 1)
            load_pair(ffn1, *ffn_w1, 0, loaded=1)
            with sp.Fori(1, PAIRS) as i:
                load_pair(ffn1, *ffn_w1, i)

            load(u_gl, column_tile(a["w_in"], slice(COL_GL, COL_GL + rank)),
                 dst=wst[u_gl % 2][:, :, 0:rank])
            tiles = [COL_VA, COL_VA + 1, COL_Q, COL_Q + 1, COL_K, COL_K + 1, COL_V, COL_V + 1,
                     COL_V + 2, COL_V + 3] + [COL_B + i for i in range(6)] + [COL_U, COL_U + 1] + \
                    [COL_R + i for i in range(heads)]
            for i, c in enumerate(tiles):
                load(u_va[0] + i, column_tile(a["w_in"], slice(c * P, c * P + P)))
                if i == 0:
                    for j in range(KT):
                        s, use = ffn1.down(j)
                        sp.wait_ge(free[s], released[s][use])
                        sp.dma_start(x_dram[:, j, :], x[:, j, :]).then_inc(spilled, 16)
                if i == 1:
                    sp.wait_ge(rs_cols, 1)
                    for m in range(GL_ROWS // rank):
                        sp.dma_start(w2[m * rank:m * rank + rank, :], a["w_gate2"][0]).then_inc(mix_in, 16)
                    for h in range(heads):
                        sp.dma_start(bias[64 * (h % 2):64 * (h % 2) + 64, h // 2, :],
                                     a["b_s"][0, h:h + 1, :].broadcast_to([64, P])).then_inc(mix_in, 16)
                    for e in range(2):
                        sp.dma_start(s_in[64 * e:64 * e + 64, :, :],
                                     a["state_gla"][0, 0].rearrange("(q e) k v -> e k q v", e=2)[e]
                                     ).then_inc(mix_in, 16)
                    sp.dma_start(ws_in[:], a["w_s"][0].rearrange("h i j -> i h j")).then_inc(ws_landed, 16)

            sp.wait_ge(s0_set, NTILE)
            sp.wait_ge(s1_set, NTILE + 1)
            sp.wait_ge(va_n_set, NTILE + 1)
            for dst, s in ((gla_prompt, s0), (gla_sample, s1)):
                for e in range(2):
                    sp.dma_start(dst[0, 0].rearrange("(q e) k v -> e k q v", e=2)[e],
                                 s[64 * e:64 * e + 64, :, :]).then_inc(state_out, 16)
            sp.dma_start(v_sample[0, 0], va_n[0:dec, :]).then_inc(state_out, 16)
            sp.wait_ge(z_set, 2)
            with nc.allow_non_contiguous_dma("two columns of z a stream, 1024 numbers in all"):
                for c in range(2):
                    for dst, end in ((conv_prompt, seq + 2), (conv_sample, ZW)):
                        sp.dma_start(dst[0, 0][:, c * P:c * P + P].rearrange("w p -> p w"),
                                     zp[:, c, end - 2:end]).then_inc(state_out, 16)
            for j in range(KT):
                load(u_wo[j], column_tile(a["w_o"], slice(j * P, j * P + P)))
                if j == 0:
                    sp.wait_ge(ya_set, 2)
                    sp.wait_ge(yb_set, 2)
                    sp.wait_ge(spilled, 16 * KT)
                    sp.dma_start(x[:], x_dram).then_inc(reloaded, 16)
            load_pair(ffn2, *ffn_w2, 0)
            sp.wait_ge(y_lo, KT)
            sp.wait_ge(state_out, 16 * N_STATE_OUT)
            sp.dma_start(pnat[:, 0:NTILE, :], a["p_prompt"][0, 0].rearrange("(t p) c -> p t c", p=P)
                         ).then_inc(p_in, 16)
            sp.dma_start(pnat[0:dec, NTILE, :], a["p_sample"][0, 0]).then_inc(p_in, 16)
            sp.dma_start(wpst[:], a["w_ple_proj"][0].rearrange("(k p) n -> p k n", p=P)).then_inc(p_in, 16)
            with sp.Fori(1, PAIRS) as i:
                load_pair(ffn2, *ffn_w2, i)
            for j in range(KT):
                load(u_ple[j], column_tile(a["w_ple_gate"], slice(j * P, j * P + P)))
                if j == 0:
                    sp.wait_ge(p_copied, NROUND)
                    sp.dma_start(g_final, a["final_norm"].rearrange("(o n) -> o n", o=1)
                                 .broadcast_to([P, d])).then_inc(gf_in, 16)
            for t in range(NTILE + 1):
                sp.wait_ge(fin_set, t + 1)
                if t < NTILE:
                    sp.dma_start(y_prompt[0, t * P:t * P + P, :], y_out(t)).then_inc(outs[t % 4], 16)
                else:
                    sp.dma_start(y_sample[0], y_out(t)[P - dec:P]).then_inc(outs[t % 4], 16)
            for b in range(4):
                sp.wait_ge(outs[b], 16 * len(range(b, NTILE + 1, 4)))
            sp.wait_ge(state_out, 16 * N_STATE_OUT)

        @block.gpsimd
        def _(pool):
            def add_squares(norm):
                for j in range(1, KT):
                    pool.wait_ge(sq_set, KT * (norm - 1) + j + 1)
                    if j > 1:
                        pool.wait_ge(sq_added, (KT - 1) * (norm - 1) + j - 1)
                    pool.tensor_tensor(acc[:], acc[:], sq[:, j % 2, :], ALU.add).then_inc(sq_added, 1)

            def silu_times_r(n_silu, n_h):
                pool.wait_ge(g_silu, n_silu)
                if n_h is not None:
                    pool.wait_ge(h_set, n_h)
                pool.tensor_tensor(sr[:], sg[:], r[:], ALU.mult).then_inc(g_silu_r, 1)

            def ffn_pairs(before):
                def pair(i):
                    n = before + i
                    first = isinstance(n, int) and n == 0
                    silu_times_r(n * 2 + 1, None if first else n * (1 + NB))
                    silu_times_r(n * 2 + 2, n * (1 + NB) + 1)
                pair(0)
                with pool.Fori(1, PAIRS) as i:
                    pair(i)

            pool.memset(ones[:], 1.0).then_inc(ones_set, 1)
            pool.memset(eps[:], EPS).then_inc(ones_set, 1)
            pool.memset(ident[:], 0.0).then_inc(ones_set, 1)
            pool.wait_ge(ones_set, 3)
            pool.affine_select(out=ident[:], in_=ident[:], compare_op=ALU.not_equal, fill=1.0, base=0,
                               pattern=[[-1, P]], channel_multiplier=1).then_inc(ones_set, 1)

            pool.wait_ge(w_hi, 1)
            half = slice(0, KT // 2)
            pool.tensor_tensor(wl[0][:, half], wst[0][:, half], wh[0][:, half].bitcast(F32), ALU.subtract
                               ).then_inc(w_lo_pool, 1)

            ffn_pairs(0)
            add_squares(1)

            pool.wait_ge(rs_cols, 1)
            pool.memset(reset[:], 1.0).then_inc(reset_set, 1)
            pool.wait_ge(reset_set, 1)
            pool.memset(reset[:].rearrange("p (b n) -> p b n", n=dec)[:, 0:T // dec:L // dec, 0:1], 0.0
                        ).then_inc(reset_set, 1)
            for m, big in ((keep_hi, 3e38), (keep_lo, -3e38)):
                pool.memset(m[:], big).then_inc(mask_set, 1)
            pool.wait_ge(mask_set, 2)
            for m in (keep_hi, keep_lo):
                pool.memset(m[0:L, L:P], 0.0).then_inc(mask_set, 1)
            pool.wait_ge(mask_set, 4)
            for m in (keep_hi, keep_lo):
                pool.affine_select(out=m[:], in_=m[:], compare_op=ALU.is_ge, fill=0.0, base=0,
                                   pattern=[[1, P]], channel_multiplier=-1).then_inc(mask_set, 1)
            pool.wait_ge(ws_landed, 16)
            pool.memset(ws_in[0:L, :, L:P], 0.0).then_inc(ws_masked, 1)
            pool.memset(ke_n[:], 0.0).then_inc(zeroed, 1)
            pool.memset(s0[:], 0.0).then_inc(zeroed, 1)
            for c in range(NPAIR):
                pool.wait_ge(e_pos, c + 1)
                pool.tensor_copy(decay[:, c, 0:2 * NTILE], mix[:, Q_ + c, L - 1:seq:L])
                pool.tensor_copy(decay[:, c, 2 * NTILE:2 * NTILE + 1], mix[:, Q_ + c, T - 1:T]
                                 ).then_inc(decay_set, 1)
                pool.wait_ge(decay_set, c + 1)
                pool.tensor_tensor(mix[:, Q_ + c, :], mix[:, Q_ + c, :], r[:], ALU.mult).then_inc(e_r, 1)
                pool.wait_ge(e_neg, c + 1)
                pool.tensor_tensor(mix[:, K_ + c, :], mix[:, K_ + c, :], r[:], ALU.mult).then_inc(e_r, 1)
            pool.wait_ge(ws_full, 1)
            pool.memset(st_q[:], 0.0).then_inc(zeroed, 1)
            pool.wait_ge(g_cum, 2)
            pool.wait_ge(ke_set, NPAIR)
            pool.wait_ge(free[SET_A], released[SET_A][g_qkv[7][1]])

            def mixers(p, e, w=P):
                t = 2 * p + e
                tok = bass.ds(t * P, w)
                if not (isinstance(t, int) and t == 1):
                    pool.wait_ge(a_full, t)
                pool.tensor_copy(st_a[:, :, 0:w], mix[:, 0:10, tok]).then_inc(st_a_set, 1)

            mixers(0, 1)
            with pool.Fori(1, NTILE // 2) as p:
                mixers(p, 0)
                mixers(p, 1)

            pool.wait_ge(a_full, NTILE + 1)
            pool.wait_ge(free[SET_A], released[SET_A][g_big[NTILE - 1][1]])
            for c in range(2):
                pool.memset(zp[:, c, 0:2], 0.0)
                first = row_of["state_conv"] + c
                pool.tensor_copy(zp[:, c, seq + 2:seq + 4], cols[:, first:first + 3:2])
                pool.tensor_tensor(zp[:, c, 2:seq + 2], late[:, 2 + c, 0:seq], late[:, 4 + c, 0:seq],
                                   ALU.mult)
                pool.tensor_tensor(zp[:, c, seq + 4:ZW], late[:, 2 + c, seq:T], late[:, 4 + c, seq:T],
                                   ALU.mult).then_inc(z_set, 1)
            def y_a(c):
                if c == 0:
                    pool.wait_ge(gm_set, NTILE + 1)
                pool.tensor_tensor(mix[:, VA + c, :], mix[:, VA + c, :], late[:, 6 + c, :], ALU.mult
                                   ).then_inc(ya_set, 1)

            def y_b(c):
                pool.wait_ge(conv_acc, 2 * c + 2)
                pool.tensor_tensor(mix[:, Q_ + c, 0:seq], cacc[:, 0:seq], late[:, c, 0:seq], ALU.mult)
                pool.tensor_tensor(mix[:, Q_ + c, seq:T], cacc[:, seq + 2:T + 2], late[:, c, seq:T],
                                   ALU.mult).then_inc(yb_set, 1)

            def y_c(h):
                pool.wait_ge(r_silu, h + 1)
                pool.wait_ge(o_normed, h + 1)
                pool.tensor_tensor(mix[:, V_ + h, :], mix[:, V_ + h, :], r_gate[:], ALU.mult
                                   ).then_inc(yc_set, 1)

            y_a(0)
            y_b(0)
            y_a(1)
            y_b(1)
            for h in range(heads - 1):
                y_c(h)
            add_squares(2)
            ffn_pairs(PAIRS)
            add_squares(3)
            for j in range(KT - 1):
                pool.wait_ge(ple_set, j + 1)
                pool.tensor_tensor(x[:, j, :], x[:, j, :], h32[:], ALU.add).then_inc(x_added, 1)

        @block.scalar
        def _(act):
            def split_hi(n, i=0, width=P):
                b = n % 2
                act.wait_ge(w_landed[b], 16 * (n // 2 + 1 + STEP // 2 * i))
                wait_used(act, n, i)
                if width == rank:
                    act.activation(rank_parts(b, 0), rank_columns(b), ACT.Copy).then_inc(w_hi, 1)
                else:
                    act.activation(wh[b][:], wst[b][:], ACT.Copy).then_inc(w_hi, 1)

            def x_square(t):
                w = P if t < NTILE else dec
                src = xin[:, t, :] if t < NTILE else xin_s[0:dec, :]
                act.wait_ge(x_in[t], 16)
                if t > 0:
                    act.wait_ge(x_sq, t)
                act.activation(sg[0:w, 0:d], src, ACT.Square, accum_out=ss[0:w, t:t + 1]).then_inc(x_sq, 1)

            def x_hi(norm, j):
                act.activation(xh[:, j, :], x[:, j, :], ACT.Copy, scale=gain(norm, j)).then_inc(xg_hi, 1)

            def square(norm, j):
                if j == 0 and norm > 1:
                    act.wait_ge(rs_cols, norm - 1)
                if j > 2:
                    act.wait_ge(sq_added, (KT - 1) * (norm - 1) + j - 2)
                act.activation(acc[:] if j == 0 else sq[:, j % 2, :], x[:, j, :], ACT.Square
                               ).then_inc(sq_set, 1)

            def norm_roots(norm):
                if norm == 0:
                    for t in range(TILE_ENDS[0] + 1, NTILE + 1):
                        x_square(t)
                    act.wait_ge(x_sq, NTILE + 1)
                    sums_ = ss
                else:
                    act.wait_ge(rs_cols, norm)
                    sums_ = ps[:, 6, :]
                act.activation(rcol[:, 0:NTILE], sums_[:, 0:NTILE], ACT.Sqrt, bias=eps[:], scale=1.0 / d)
                act.activation(rcol[0:dec, NTILE:NTILE + 1], sums_[0:dec, NTILE:NTILE + 1], ACT.Sqrt,
                               bias=eps[0:dec], scale=1.0 / d).then_inc(rms_set, 1)

            def norm_copies(norm):
                act.wait_ge(r_full, norm + 1)
                act.activation(r[:, 0:seq].rearrange("p (b n) -> p b n", b=2), ps[:, 6:8, :], ACT.Copy)
                act.activation(r[:, seq:T], r_sample, ACT.Copy).then_inc(r_set, 1)

            def silu(f, q, i, k):
                act.wait_ge(free[SET_A], at_step(released[SET_A][f.a + q], i))
                if not (isinstance(k, int) and k == 0):
                    act.wait_ge(g_silu_r, k)
                act.activation(sg[:], tg[:], ACT.Silu).then_inc(g_silu, 1)

            def h_part(n, q, cols_):
                act.wait_ge(h_set, n)
                act.activation(hh[:, q, cols_], h32[:, cols_], ACT.Copy).then_inc(h_hi, 1)

            def ffn(f, before, norm, extra=None):
                def pair(i, first=False, last=False):
                    n = f.unit
                    k = before + i
                    split_hi(n + 1, i)
                    if first:
                        norm_roots(norm)
                        split_hi(n + 2, i)
                        norm_copies(norm)
                    if last and extra:
                        extra()
                    silu(f, 0, i, 2 * k)
                    if not first:
                        split_hi(n + 2, i)
                    h_part((1 + NB) * k + 1, 0, slice(0, T))
                    split_hi(n + 3, i)
                    silu(f, 1, i, 2 * k + 1)
                    split_hi(n + 4, i)
                    for blk in range(NB):
                        h_part((1 + NB) * k + 2 + blk, 1, slice(blk * TB, blk * TB + TB))
                    split_hi(n + 5, i)
                    for j in range(KT if last else 0):
                        if j == KT // 2:
                            split_hi(n + 6, i, rank if norm == 0 else P)
                        s, use = f.down(j)
                        act.wait_ge(free[s], released[s][use])
                        square(norm + 1, j)
                        x_hi(norm + 1, j)
                    if not last:
                        split_hi(n + 6, i)
                return pair

            def p_copies():
                for g in range(NROUND):
                    act.wait_ge(p_full, g + 1)
                    w = min(4 * P, T - 4 * P * g)
                    act.activation(p_t[:, :, 4 * P * g:4 * P * g + w], ps[:, 6:8, 0:w], ACT.Copy
                                   ).then_inc(p_copied, 1)

            for t in range(TILE_ENDS[0]):
                x_square(t)
            copied = 0
            for blk in range(NB):
                for t in range(copied, TILE_ENDS[blk]):
                    if t in BY_ACT:
                        act.wait_ge(xt_full, t + 1)
                        act.activation(x[:, :, rows_of(t)], x_ps(t)[:, :, 0:rows_of(t).stop - t * P],
                                       ACT.Copy).then_inc(xt_act, 1)
                copied = TILE_ENDS[blk]
                if blk == 0:
                    split_hi(ffn1.unit)
                    act.wait_ge(cols_set, 1)
                if blk == NB - 1:
                    x_square(TILE_ENDS[0])
                wait_copied(act, copied)
                cs = slice(blk * TB, blk * TB + TB)
                for j in range(KT):
                    act.activation(xh[:, j, cs], x[:, j, cs], ACT.Copy, scale=gain(0, j)).then_inc(xg_hi, 1)
            pair = ffn(ffn1, 0, 0)
            pair(0, first=True)
            with act.Fori(1, PAIRS - 1) as i:
                pair(i)
            pair(PAIRS - 1, last=True)

            split_hi(u_va[0])
            norm_roots(1)
            split_hi(u_va[1])
            norm_copies(1)
            act.wait_ge(mix_in, 16 * N_MIX_IN)
            act.activation(w2_parts, w2[0:GL_ROWS, :], ACT.Copy).then_inc(w2_set, 1)
            act.wait_ge(free[g_gl[0]], released[g_gl[0]][g_gl[1]])
            act.activation(gl_parts, gl, ACT.Copy).then_inc(gl_set, 1)
            split_hi(u_qkv[0])
            for c in range(NPAIR):
                s, use = g_z[c]
                act.wait_ge(full[s], use + 1)
                act.activation(mix[:, KE + c, :].rearrange("p (b n) -> p b n", b=NB), banks(s), ACT.Abs,
                               bias=cols[:, row_of["b_gate2"] + c:row_of["b_gate2"] + c + 1]
                               ).then_inc(z_abs, 1)
                act.wait_ge(z_abs, c + 1)
                act.activation(mix[:, KE + c, :], mix[:, KE + c, :], ACT.Exp, scale=-1.0).then_inc(z_exp, 1)
                act.wait_ge(z_exp, c + 1)
                act.activation(mix[:, KE + c, :], mix[:, KE + c, :], ACT.Ln, bias=ones[:, 0:1]
                               ).then_inc(z_log, 1)
                if c == 0:
                    split_hi(u_qkv[1])
            split_hi(u_qkv[2])
            for c in range(NPAIR):
                act.wait_ge(g_cum, c + 1)
                act.activation(mix[:, Q_ + c, :], mix[:, KE + c, :], ACT.Exp, scale=1.0 / TAU
                               ).then_inc(e_pos, 1)
                act.activation(mix[:, K_ + c, :], mix[:, KE + c, :], ACT.Exp, scale=-1.0 / TAU
                               ).then_inc(e_neg, 1)
            for u in u_qkv[3:]:
                split_hi(u)
            split_hi(u_big[0])

            def mixers(p, e, w=P):
                t = 2 * p + e
                first = isinstance(t, int) and t == 0
                if first:
                    act.wait_ge(zeroed, 3)
                    act.wait_ge(free[SET_B], released[SET_B][g_qkv[0][1]])
                    act.wait_ge(free[SET_A], released[SET_A][g_qkv[1][1]])
                else:
                    act.wait_ge(o_full, t)
                for m in range(2):
                    last = act.activation(st_q[64 * m:64 * m + 64, m:heads:2, 0:w],
                                          mix[64 * m:64 * m + 64, Q_:Q_ + 2, bass.ds(t * P, w)], ACT.Copy)
                last.then_inc(st_q_set, 1)
                n = u_big[0] + 1 + e
                act.wait_ge(w_landed[n % 2], 16 * (n // 2 + 1 + p))
                act.wait_ge(full[SET_A], g_big[0][1] + t)
                act.activation(wh[n % 2][:], wst[n % 2][:], ACT.Copy).then_inc(w_hi, 1)
                act.wait_ge(tile_t, t + 1)
                if not first:
                    act.wait_ge(o_full, t)
                act.activation(v_n[0:w, :], ps[0:w, 3, :], ACT.Copy).then_inc(v_n_set, 1)
                act.wait_ge(ln_mean, t + 1)
                act.activation(ln[0:w, 8:9], ln[0:w, 7:8], ACT.Sqrt, bias=eps[0:w]).then_inc(ln_root, 1)
                act.wait_ge(o_full, t + 1)
                act.activation(mix[:, V_:V_ + heads, bass.ds(t * P, w)],
                               ps[:, 6, :].rearrange("p (h i) -> p h i", h=heads)[:, :, 0:w], ACT.Copy
                               ).then_inc(o_set, 1)

            over_token_tiles(act, mixers)

            def o_square(h):
                if h > 0:
                    act.wait_ge(os_cols, h)
                act.activation(osq[:], mix[:, V_ + h, :], ACT.Square).then_inc(osq_set, 1)

            def o_roots():
                act.wait_ge(os_cols, heads)
                by_head = [t.rearrange("p (h t) -> p h t", h=heads)
                           for t in (rcol[:], ps[:, 6, 0:heads * (NTILE + 1)])]
                act.activation(by_head[0][:, :, 0:NTILE], by_head[1][:, :, 0:NTILE], ACT.Sqrt,
                               bias=eps[:], scale=1.0 / dv)
                act.activation(by_head[0][0:dec, :, NTILE], by_head[1][0:dec, :, NTILE], ACT.Sqrt,
                               bias=eps[0:dec], scale=1.0 / dv).then_inc(orms_set, 1)

            def conv_first(c):
                act.wait_ge(z_set, c + 1)
                if c > 0:
                    act.wait_ge(yb_set, c)
                tap = row_of["conv_w"] + c
                act.activation(cacc, zp[:, c, 0:ZW - 2], ACT.Copy, scale=cols[:, tap:tap + 1]
                               ).then_inc(conv_begun, 1)

            def gate_silu(h):
                s, use = g_r[h]
                act.wait_ge(free[s], released[s][use])
                act.activation(r_gate[:], r_gate[:], ACT.Silu).then_inc(r_silu, 1)

            def y_part(k):
                if k < KT - 1:
                    act.wait_ge(xh_used, k + 1)
                else:
                    act.wait_ge(full[g_r[3][0]], g_r[3][1] + 1)
                if k < 2:
                    act.wait_ge(ya_set, k + 1)
                elif k < 4:
                    act.wait_ge(yb_set, k - 1)
                elif k < KT - 1:
                    act.wait_ge(yc_set, k - 3)
                else:
                    act.wait_ge(yc_last, 1)
                act.activation(xh[:, k, :], y_of(k), ACT.Copy).then_inc(y_hi, 1)

            act.wait_ge(o_set, NTILE + 1)
            act.wait_ge(g_cum, 2)
            o_square(0)
            o_square(1)
            conv_first(0)
            split_hi(u_r[2])
            o_square(2)
            o_square(3)
            o_roots()
            gate_silu(0)
            split_hi(u_r[3])
            conv_first(1)
            gate_silu(1)
            split_hi(u_wo[0])
            y_part(0)
            gate_silu(2)
            for k in range(1, KT - 1):
                y_part(k)
            split_hi(u_wo[1])
            gate_silu(3)
            y_part(KT - 1)

            for j in range(KT):
                if j < KT - 1:
                    if j > 0:
                        split_hi(u_wo[j + 1])
                else:
                    split_hi(ffn2.unit)
                    for k in range(KT - 1):
                        act.wait_ge(xh_used, KT - 1 + k + 1)
                        x_hi(2, k)
                s, use = g_wo[j]
                act.wait_ge(free[s], released[s][use])
                square(2, j)
            x_hi(2, KT - 1)
            pair = ffn(ffn2, PAIRS, 2, p_copies)
            pair(0, first=True)
            act.wait_ge(p_in, 48)
            act.activation(wph[:], wpst[:], ACT.Copy).then_inc(wp_hi, 1)
            with act.Fori(1, PAIRS - 1) as i:
                pair(i)
            pair(PAIRS - 1, last=True)

            for c in range(2):
                act.activation(hh[:, c, :], p_t[:, c, :], ACT.Copy).then_inc(p_hi, 1)
            for j in range(KT):
                if j == 0:
                    norm_roots(3)
                if j < KT - 1:
                    split_hi(u_ple[j + 1])
                if j == 0:
                    norm_copies(3)
                if j < KT - 1:
                    act.wait_ge(free[SET_A], released[SET_A][g_gate[j][1]])
                    if j > 0:
                        act.wait_ge(ple_set, j)
                    act.activation(sg[:], tg[:], ACT.Sigmoid).then_inc(gate_sig, 1)

            def last_sigmoid(blk):
                cs = slice(blk * TB, blk * TB + TB)
                if blk == 0:
                    act.wait_ge(ple_set, KT - 1)
                act.wait_ge(last_scaled, blk + 1)
                act.activation(sg[:, cs], tg[:, cs], ACT.Sigmoid).then_inc(last_sig, 1)

            def token_square(t):
                rs = fin_row(t)
                act.wait_ge(fin_full, t + 1)
                if t > 0:
                    act.wait_ge(fin_sq, t)
                act.activation(sr[rs, 0:d], fin_ps(t)[rs], ACT.Square, accum_out=ss[rs, t:t + 1]
                               ).then_inc(fin_sq, 1)

            def token_root(t):
                rs = fin_row(t)
                act.wait_ge(fin_sq, t + 1)
                act.activation(rcol[rs, t:t + 1], ss[rs, t:t + 1], ACT.Sqrt, bias=eps[rs], scale=1.0 / d
                               ).then_inc(fin_root, 1)

            last_sigmoid(0)
            last_sigmoid(1)
            for t in FIN_TILES[0]:
                token_square(t)
            for t in FIN_TILES[0]:
                token_root(t)
            token_square(FIN_TILES[1][0])
            last_sigmoid(2)
            for t in range(FIN_TILES[1][0], NTILE):
                token_root(t)
                token_square(t + 1)
            token_root(NTILE)

        @block.vector
        def _(dve):
            def split_lo(n, i=0, width=P):
                b = n % 2
                dve.wait_ge(w_hi, at_step(n + 1, i))
                if width == rank:
                    dve.tensor_tensor(rank_parts(b, 1), rank_columns(b), rank_parts(b, 0).bitcast(F32),
                                      ALU.subtract).then_inc(w_lo, 1)
                else:
                    dve.tensor_tensor(wl[b][:], wst[b][:], wh[b][:].bitcast(F32), ALU.subtract
                                      ).then_inc(w_lo, 1)

            def x_lo(norm, j):
                dve.wait_ge(xg_hi, xg_before(norm) + j + 1)
                dve.scalar_tensor_tensor(xl[:, j, :], x[:, j, :], gain(norm, j), xh[:, j, :].bitcast(F32),
                                         ALU.mult, ALU.subtract).then_inc(xg_lo, 1)

            def finish_norm(norm):
                dve.wait_ge(rms_set, norm + 1)
                dve.reciprocal(ricol[:, 0:NTILE], rcol[:, 0:NTILE])
                dve.reciprocal(ricol[0:dec, NTILE:NTILE + 1], rcol[0:dec, NTILE:NTILE + 1]
                               ).then_inc(inv_set, 1)

            def ffn(f, before, norm):
                def pair(i, first=False, last=False):
                    n = f.unit
                    k = before + i
                    nh = (1 + NB) * k

                    def scale_gate(q):
                        dve.wait_ge(full[SET_A], at_step(f.a + q + 1, i))
                        if not (isinstance(k, int) and k == 0 and q == 0):
                            dve.wait_ge(g_silu, 2 * k + q)
                        dve.tensor_tensor(blocks(tg[:]), banks(SET_A), blocks(r[:]), ALU.mult
                                          ).then_inc(free[SET_A], 1)

                    def h_lo_part(m, q, cs):
                        dve.wait_ge(h_hi, nh + m)
                        dve.tensor_tensor(hl[:, q, cs], h32[:, cs], hh[:, q, cs].bitcast(F32),
                                          ALU.subtract).then_inc(h_lo, 1)

                    split_lo(n + 1, i)
                    if first:
                        finish_norm(norm)
                        split_lo(n + 2, i)
                        dve.wait_ge(r_set, norm + 1)
                    scale_gate(0)
                    if not first:
                        split_lo(n + 2, i)
                    dve.wait_ge(full[SET_B], at_step(f.b + 1, i))
                    dve.wait_ge(g_silu_r, 2 * k + 1)
                    dve.tensor_tensor(blocks(h32[:]), banks(SET_B), blocks(sr[:]), ALU.mult
                                      ).then_inc(h_set, 1)
                    split_lo(n + 3, i)
                    h_lo_part(1, 0, slice(0, T))
                    scale_gate(1)
                    split_lo(n + 4, i)
                    for blk in range(NB):
                        cs = slice(blk * TB, blk * TB + TB)
                        if blk < NB - 1:
                            dve.wait_ge(up_block, (NB - 1) * k + blk + 1)
                        else:
                            dve.wait_ge(full[SET_B], at_step(f.b + 2, i))
                        if blk == 0:
                            dve.wait_ge(g_silu_r, 2 * k + 2)
                        dve.tensor_tensor(h32[:, cs], ps[:, SETS[SET_B] + blk, 0:TB], sr[:, cs], ALU.mult
                                          ).then_inc(h_set, 1)
                        h_lo_part(2 + blk, 1, cs)
                    split_lo(n + 5, i)
                    for j in range(KT):
                        if j == (KT - 2 if last else KT // 2):
                            split_lo(n + 6, i, rank if last and norm == 0 else P)
                        s = j % 2
                        dve.wait_ge(full[s], at_step((f.a, f.b)[s] + 3 + j // 2, i))
                        if i is not None and not first:
                            dve.wait_ge(free[s], at_step(released[s][f.down(j, 0)[1]] - RELEASES[s], i,
                                                         RELEASES[s]))
                        dve.scalar_tensor_tensor(blocks(x[:, j, :]), banks(s), 0.5, blocks(x[:, j, :]),
                                                 ALU.mult, ALU.add).then_inc(free[s], 1)
                        if last and j > 0:
                            x_lo(norm + 1, j - 1)
                    if last:
                        x_lo(norm + 1, KT - 1)
                return pair

            copied = 0
            for blk in range(NB):
                for t in range(copied, TILE_ENDS[blk]):
                    if t not in BY_ACT:
                        dve.wait_ge(xt_full, t + 1)
                        dve.tensor_copy(x[:, :, rows_of(t)], x_ps(t)[:, :, 0:rows_of(t).stop - t * P]
                                        ).then_inc(xt_dve, 1)
                    if t == 0:
                        dve.wait_ge(rows_t, 1)
                        dve.tensor_copy(cols[:, 0:KT], ps[:, 7, 0:KT]).then_inc(cols_set, 1)
                copied = TILE_ENDS[blk]
                if blk == 0:
                    dve.wait_ge(w_hi, 1)
                    half = slice(KT // 2, KT)
                    dve.tensor_tensor(wl[0][:, half], wst[0][:, half], wh[0][:, half].bitcast(F32),
                                      ALU.subtract).then_inc(w_lo, 1)
                wait_copied(dve, copied)
                cs = slice(blk * TB, blk * TB + TB)
                for j in range(KT):
                    dve.wait_ge(xg_hi, KT * blk + j + 1)
                    if blk == 0 and j == 0:
                        dve.wait_ge(cols_set, 1)
                    dve.scalar_tensor_tensor(xl[:, j, cs], x[:, j, cs], gain(0, j), xh[:, j, cs].bitcast(F32),
                                             ALU.mult, ALU.subtract).then_inc(xg_lo, 1)
                    if (blk, j) == (1, 4):
                        dve.wait_ge(rows_t, 2)
                        dve.tensor_copy(cols[:, KT:n_rows], ps[:, 7, KT:n_rows]).then_inc(cols_set, 1)
            pair = ffn(ffn1, 0, 0)
            pair(0, first=True)
            with dve.Fori(1, PAIRS - 1) as i:
                pair(i)
            pair(PAIRS - 1, last=True)

            def result(use):
                s, u = use
                dve.wait_ge(full[s], u + 1)
                return banks(s)

            def keep(use, slot):
                src = result(use)
                dve.tensor_tensor(blocks(mix[:, slot, :]), src, blocks(r[:]), ALU.mult
                                  ).then_inc(free[use[0]], 1)

            split_lo(u_va[0])
            finish_norm(1)
            split_lo(u_va[1])
            dve.wait_ge(r_set, 2)
            s, use = g_gl
            dve.wait_ge(full[s], use + 1)
            dve.tensor_tensor(blocks(gl), banks(s)[0:GL_ROWS], blocks(r[0:GL_ROWS]), ALU.mult
                              ).then_inc(free[s], 1)
            dve.wait_ge(w2_set, 1)
            rows_ = slice(2 * GLW, 3 * GLW)
            dve.tensor_tensor(w2_parts[rows_], w2[rows_, :], w2_parts[rows_].bitcast(F32), ALU.subtract
                              ).then_inc(w2_low, 1)
            dve.wait_ge(gl_set, 1)
            rows_ = slice(GLW, 2 * GLW)
            dve.tensor_tensor(gl_parts[rows_], gl[rows_], gl_parts[rows_].bitcast(F32), ALU.subtract
                              ).then_inc(gl_low, 1)
            split_lo(u_qkv[0])

            def z_min(c):
                s, use = g_z[c]
                dve.wait_ge(z_abs, c + 1)
                dve.tensor_scalar(blocks(mix[:, K_ + c, :]), banks(s),
                                  cols[:, row_of["b_gate2"] + c:row_of["b_gate2"] + c + 1], 0.0,
                                  ALU.add, ALU.min).then_inc(free[s], 1)

            keep(g_va[0], VA)
            z_min(0)
            keep(g_va[1], VA + 1)
            split_lo(u_qkv[1])
            dve.wait_ge(ws_full, 1)
            dve.tensor_copy(ws_t[:], ps[:, 6, :].rearrange("p (h i) -> p h i", h=heads)).then_inc(ws_set, 1)
            z_min(1)
            dve.wait_ge(reset_set, 2)
            for c in range(NPAIR):
                s, use = g_z[c]
                dve.wait_ge(z_log, c + 1)
                dve.wait_ge(free[s], released[s][use])
                dve.tensor_tensor(mix[:, K_ + c, :], mix[:, K_ + c, :], mix[:, KE + c, :], ALU.subtract
                                  ).then_inc(ls_set, 1)
                dve.wait_ge(ls_set, c + 1)
                dve.tensor_tensor_scan(mix[:, KE + c, :], reset[:], mix[:, K_ + c, :], 0.0,
                                       ALU.mult, ALU.add).then_inc(g_cum, 1)
            split_lo(u_qkv[2])
            for c in range(NPAIR):
                dve.wait_ge(e_r, 2 * c + 1)
                src = result(g_qkv[c])
                dve.scalar_tensor_tensor(blocks(mix[:, Q_ + c, :]), src, float(dk) ** -0.5,
                                         blocks(mix[:, Q_ + c, :]), ALU.mult, ALU.mult
                                         ).then_inc(free[g_qkv[c][0]], 1)
                split_lo(u_qkv[3 + c])
            for c in range(NPAIR):
                dve.wait_ge(e_r, 2 * c + 2)
                s, use = g_qkv[2 + c]
                src = result(g_qkv[2 + c])
                dve.tensor_tensor(blocks(mix[:, K_ + c, :]), src, blocks(mix[:, K_ + c, :]), ALU.mult
                                  ).then_inc(free[s], 1)
                dve.wait_ge(free[s], released[s][use])
                dve.tensor_tensor(mix[:, KE + c, 0:seq].rearrange("p (b n) -> p b n", n=L),
                                  mix[:, K_ + c, 0:seq].rearrange("p (b n) -> p b n", n=L),
                                  decay[:, c, 0:2 * NTILE].unsqueeze(2).broadcast_to([P, 2 * NTILE, L]),
                                  ALU.mult)
                dve.tensor_scalar(mix[:, KE + c, seq:T], mix[:, K_ + c, seq:T],
                                  decay[:, c, 2 * NTILE:2 * NTILE + 1], None, ALU.mult).then_inc(ke_set, 1)
                split_lo(u_qkv[5 + c])
            for v in range(heads):
                keep(g_qkv[4 + v], V_ + v)
                if v == 0:
                    split_lo(u_qkv[7])
                if v == 1:
                    split_lo(u_big[0])

            def mixers(p, e, w=P):
                t = 2 * p + e
                first = isinstance(t, int) and t == 0
                sample = w < P
                nblk = 1 if sample else 2
                n = u_big[0] + 1 + e
                dve.wait_ge(w_hi, n + 1 + 2 * p)
                dve.tensor_tensor(wl[n % 2][:], wst[n % 2][:], wh[n % 2][:].bitcast(F32), ALU.subtract
                                  ).then_inc(w_lo, 1)
                va = ps[0:w, 4, 2 * P:4 * P]
                dve.wait_ge(tile_t, t + 1)
                if not first:
                    dve.wait_ge(va_n_set, t)
                dve.bn_stats(ln[0:w, 0:6], va).then_inc(ln_stat, 1)
                if first:
                    dve.wait_ge(zeroed, 2)
                else:
                    dve.wait_ge(ds_full, t)
                dve.wait_ge(ln_stat, t + 1)
                for m in range(nblk):
                    rs = slice(L * m, min(L * m + L, w))
                    last = dve.tensor_copy(ke_n[rs, m, :], ps[rs, 4, 0:2 * P])
                last.then_inc(ke_n_set, 1)
                dve.bn_aggr(ln[0:w, 6:8], ln[0:w, 0:6]).then_inc(ln_mean, 1)
                dve.wait_ge(ln_root, t + 1)
                dve.reciprocal(ln[0:w, 9:10], ln[0:w, 8:9]).then_inc(ln_inv, 1)
                dve.wait_ge(ln_inv, t + 1)
                if not first:
                    dve.wait_ge(gm_full, t)
                dve.tensor_scalar(va_n[0:w, :], va, ln[0:w, 6:7], ln[0:w, 9:10], ALU.subtract, ALU.mult
                                  ).then_inc(va_n_set, 1)
                if not first:
                    dve.wait_ge(o_full, t)
                dve.wait_ge(a_full, t + 1)
                dve.tensor_tensor(a_t[0:w, :, 0:w],
                                  ps[:, 5, :].rearrange("p (h i) -> p h i", h=heads)[0:w, :, 0:w],
                                  keep_hi[0:w, 0:w].unsqueeze(1).broadcast_to([w, heads, w]), ALU.min
                                  ).then_inc(a_bounded, 1)
                dve.wait_ge(a_bounded, t + 1)
                dve.tensor_tensor(a_t[0:w, :, 0:w], a_t[0:w, :, 0:w],
                                  keep_lo[0:w, 0:w].unsqueeze(1).broadcast_to([w, heads, w]), ALU.max
                                  ).then_inc(a_masked, 1)
                before = s_in if sample else s0
                dve.wait_ge(ds_full, t + 1)
                if not first:
                    dve.wait_ge(o_full, t)
                    dve.wait_ge(s0_set, min(t, NTILE) if isinstance(t, int) else t)
                for c in range(NPAIR):
                    last = dve.scalar_tensor_tensor(s1[:, c, :], before[:, c, :],
                                                    decay[:, c, bass.ds(2 * t, 1)],
                                                    ps[:, 7, c * P:c * P + P], ALU.mult, ALU.add)
                last.then_inc(s1_set, 1)
                dve.wait_ge(gm_full, t + 1)
                dve.tensor_tensor(mix[:, VA:VA + 2, bass.ds(t * P, w)],
                                  ps[:, 3, 0:2 * P].rearrange("p (c n) -> p c n", c=2)[:, :, 0:w],
                                  bias[:, :, 0:w], ALU.add).then_inc(gm_set, 1)
                if not sample:
                    dve.wait_ge(o_full, t + 1)
                    dve.wait_ge(s1_set, t + 1)
                    for c in range(NPAIR):
                        last = dve.scalar_tensor_tensor(s0[:, c, :], s1[:, c, :],
                                                        decay[:, c, bass.ds(2 * t + 1, 1)],
                                                        ps[:, 7, 2 * P + c * P:3 * P + c * P],
                                                        ALU.mult, ALU.add)
                    last.then_inc(s0_set, 1)
                    dve.wait_ge(full[SET_A], g_big[0][1] + 1 + t)
                    dve.tensor_tensor(blocks(late[:, bass.ds(t, 1), :].rearrange("p a n -> p (a n)")),
                                      banks(SET_A), blocks(r[:]), ALU.mult).then_inc(free[SET_A], 1)

            dve.wait_ge(spilled, 16 * KT)
            dve.wait_ge(mix_in, 16 * N_MIX_IN)
            dve.wait_ge(mask_set, 6)
            over_token_tiles(dve, mixers)

            def scale_r(h):
                src = result(g_r[h])
                if h > 0:
                    dve.wait_ge(yc_set, h)
                else:
                    dve.wait_ge(o_full, NTILE + 1)
                dve.tensor_tensor(blocks(r_gate[:]), src, blocks(r[:]), ALU.mult
                                  ).then_inc(free[g_r[h][0]], 1)

            def o_invert():
                dve.wait_ge(orms_set, 1)
                by_head = [t[:].rearrange("p (h t) -> p h t", h=heads) for t in (ricol, rcol)]
                dve.reciprocal(by_head[0][:, :, 0:NTILE], by_head[1][:, :, 0:NTILE])
                dve.reciprocal(by_head[0][0:dec, :, NTILE], by_head[1][0:dec, :, NTILE]
                               ).then_inc(oinv_set, 1)

            def o_gain(h):
                return cols[:, row_of["gla_norm"] + h:row_of["gla_norm"] + h + 1]

            def o_norm_samples():
                dve.wait_ge(or_samples, 1)
                for h in range(heads):
                    o_ = mix[:, V_ + h, seq:T]
                    dve.scalar_tensor_tensor(o_, or_sample(h), o_gain(h), o_, ALU.mult, ALU.mult)

            def o_norm(h):
                dve.wait_ge(or_full, h + 1)
                o_ = mix[:, V_ + h, 0:seq].rearrange("p (b n) -> p b n", b=2)
                dve.scalar_tensor_tensor(o_, ps[:, 6:8, :], o_gain(h), o_, ALU.mult, ALU.mult
                                         ).then_inc(o_normed, 1)

            def conv(c):
                dve.wait_ge(conv_begun, c + 1)
                for m in range(1, 3):
                    if m > 1:
                        dve.wait_ge(conv_acc, 2 * c + m - 1)
                    tap = row_of["conv_w"] + 2 * m + c
                    dve.scalar_tensor_tensor(cacc, zp[:, c, m:m + ZW - 2], cols[:, tap:tap + 1], cacc,
                                             ALU.mult, ALU.add).then_inc(conv_acc, 1)

            def y_part(k):
                dve.wait_ge(y_hi, k + 1)
                dve.tensor_tensor(xl[:, k, :], y_of(k), xh[:, k, :].bitcast(F32), ALU.subtract
                                  ).then_inc(y_lo, 1)

            scale_r(0)
            conv(0)
            split_lo(u_r[2])
            o_invert()
            split_lo(u_r[3])
            conv(1)
            o_norm_samples()
            o_norm(0)
            scale_r(1)
            o_norm(1)
            o_norm(2)
            scale_r(2)
            split_lo(u_wo[0])
            for k in range(4):
                y_part(k)
            o_norm(3)
            for k in range(4, KT - 1):
                y_part(k)
            scale_r(3)
            split_lo(u_wo[1])
            dve.wait_ge(r_silu, heads)
            dve.tensor_tensor(mix[:, V_ + heads - 1, :], mix[:, V_ + heads - 1, :], r_gate[:], ALU.mult
                              ).then_inc(yc_last, 1)
            y_part(KT - 1)
            dve.wait_ge(reloaded, 16)
            for j in range(KT):
                if 0 < j < KT - 1:
                    split_lo(u_wo[j + 1])
                if j == KT - 1:
                    split_lo(ffn2.unit)
                    for k in range(KT - 2):
                        x_lo(2, k)
                src = result(g_wo[j])
                dve.tensor_tensor(blocks(x[:, j, :]), src, blocks(x[:, j, :]), ALU.add
                                  ).then_inc(free[g_wo[j][0]], 1)
            for k in range(KT - 2, KT):
                x_lo(2, k)
            pair = ffn(ffn2, PAIRS, 2)
            pair(0, first=True)
            dve.wait_ge(wp_hi, 1)
            dve.tensor_tensor(wpl[:], wpst[:], wph[:].bitcast(F32), ALU.subtract).then_inc(wp_lo, 1)
            with dve.Fori(1, PAIRS - 1) as i:
                pair(i)
            pair(PAIRS - 1, last=True)

            for c in range(2):
                dve.wait_ge(p_hi, c + 1)
                dve.tensor_tensor(hl[:, c, :], p_t[:, c, :], hh[:, c, :].bitcast(F32), ALU.subtract
                                  ).then_inc(p_lo, 1)
            for j in range(KT):
                if j == 0:
                    finish_norm(3)
                if j < KT - 1:
                    split_lo(u_ple[j + 1])
                if j == 0:
                    dve.wait_ge(r_set, 4)
                if j == KT - 1:
                    continue
                src = result(g_gate[j])
                if j > 0:
                    dve.wait_ge(gate_sig, j)
                dve.tensor_tensor(blocks(tg[:]), src, blocks(r[:]), ALU.mult).then_inc(free[SET_A], 1)
                src = result(g_proj[j])
                dve.wait_ge(gate_sig, j + 1)
                if j > 0:
                    dve.wait_ge(x_added, j)
                dve.tensor_tensor(blocks(h32[:]), src, blocks(sg[:]), ALU.mult).then_inc(ple_set, 1)

            def last_gate_scaled(blk):
                cs = slice(blk * TB, blk * TB + TB)
                dve.wait_ge(last_gate, blk + 1)
                if blk == 0:
                    dve.wait_ge(gate_sig, KT - 1)
                dve.tensor_tensor(tg[:, cs], ps[:, 2 * blk, 0:TB], r[:, cs], ALU.mult
                                  ).then_inc(last_scaled, 1)

            def last_tile_added(blk):
                cs = slice(blk * TB, blk * TB + TB)
                dve.wait_ge(last_proj, blk + 1)
                dve.wait_ge(last_sig, blk + 1)
                if blk == 0:
                    dve.wait_ge(x_added, KT - 1)
                dve.tensor_tensor(h32[:, cs], ps[:, 2 * blk + 1, 0:TB], sg[:, cs], ALU.mult
                                  ).then_inc(last_ple, 1)
                dve.wait_ge(last_ple, blk + 1)
                dve.tensor_tensor(x[:, KT - 1, cs], x[:, KT - 1, cs], h32[:, cs], ALU.add
                                  ).then_inc(last_added, 1)

            def y_inverse(t):
                rs = fin_row(t)
                dve.wait_ge(fin_root, t + 1)
                dve.reciprocal(ricol[rs, t:t + 1], rcol[rs, t:t + 1]).then_inc(fin_inv, 1)

            def y_rows(t):
                rs = fin_row(t)
                dve.wait_ge(fin_inv, t + 1)
                if t > 3:
                    dve.wait_ge(outs[t % 4], 16 * (t // 4))
                dve.scalar_tensor_tensor(y_out(t)[rs].rearrange("p (b n) -> p b n", b=2), fin_ps(t)[rs],
                                         ricol[rs, t:t + 1], g_final[rs].rearrange("p (b n) -> p b n", b=2),
                                         ALU.mult, ALU.mult).then_inc(fin_set, 1)

            for blk in range(NB):
                last_gate_scaled(blk)
                last_tile_added(blk)
                if blk == 1:
                    dve.wait_ge(gf_in, 16)
                    for t in FIN_TILES[0]:
                        y_inverse(t)
                    for t in FIN_TILES[0]:
                        y_rows(t)
            for t in range(FIN_TILES[1][0], NTILE + 1):
                y_inverse(t)
                y_rows(t)

        @block.tensor
        def _(pe):
            def wait_free(s, use, i=0):
                if isinstance(i, int) and i == 0:
                    if use > 0:
                        pe.wait_ge(free[s], released[s][use - 1])
                else:
                    step = RELEASES[s]
                    pe.wait_ge(free[s], at_step(released[s][use - 1 + STEP] - step, i, step))

            def three_passes(out, w_hi_, w_lo_, x_hi_, x_lo_, blks, start, stop):
                for w_, x_ in ((w_hi_, x_hi_), (w_hi_, x_lo_), (w_lo_, x_hi_)):
                    for blk in blks:
                        last = pe.matmul(out(blk), w_, x_[:, blk * TB:blk * TB + TB],
                                         start=start and w_ is w_hi_ and x_ is x_hi_,
                                         stop=stop and w_ is w_lo_)
                return last

            def project(n, s, i=0, ready=None, hooks={}, by_block=None, tell_used=False):
                pe.wait_ge(w_lo, at_step(n + 1, i))
                b = n % 2

                def tile(k, blks):
                    return three_passes(lambda blk: ps[:, SETS[s] + blk, 0:TB], wh[b][:, k, :],
                                        wl[b][:, k, :], xh[:, k, :], xl[:, k, :], blks, k == 0, k == KT - 1)

                if by_block is not None:
                    for blk in range(NB):
                        for k in range(KT):
                            last = tile(k, (blk,))
                        last.then_inc(up_block if blk < NB - 1 else full[s], 1)
                    return
                for k in range(KT):
                    if ready is not None:
                        pe.wait_ge(ready[0], ready[1] + k + 1)
                    last = tile(k, range(NB))
                    if k == KT - 1:
                        last.then_inc(full[s], 1)
                    elif tell_used:
                        last.then_inc(xh_used, 1)
                    if k in hooks:
                        hooks[k]()

            def sums(column_sums, rows_sem, rows_val, signal, c0=0):
                pe.wait_ge(rows_sem, rows_val)
                for t in range(NTILE + 1):
                    w = P if t < NTILE else dec
                    last = pe.matmul(ps[0:w, 6, c0 + t:c0 + t + 1], column_sums[:, t * P:t * P + w],
                                     ones[:, 0:1], start=True, stop=True)
                last.then_inc(signal, 1)

            def across(out, inv, c):
                w = out.shape[1]
                return pe.matmul(out, inv[0:w, c:c + 1].broadcast_to([w, P]), ident[0:w, 0:w],
                                 start=True, stop=True)

            def spread(c0, signal):
                for t in range(NTILE):
                    last = across(ps[:, 6 + t // 4, t % 4 * P:t % 4 * P + P], ricol, c0 + t)
                last.then_inc(signal, 1)

            def norm_sums(norm):
                sums(acc, sq_added, (KT - 1) * norm, rs_cols)

            def norm_spread(norm):
                pe.wait_ge(inv_set, norm + 1)
                across(r_sample, ricol, NTILE)
                spread(0, r_full)

            def ffn(f, before, norm, last_hooks={}):
                def pair(i, first=False, last=False):
                    k = before + i
                    nh = (1 + NB) * k
                    n = f.unit
                    if not (first and norm == 0):
                        wait_free(SET_A, f.a, i)
                        project(n, SET_A, i, (xg_lo, xg_before(norm)) if first else None,
                                {6: lambda: norm_sums(norm)} if first else last_hooks if last else {})
                    wait_free(SET_B, f.b, i)
                    project(n + 1, SET_B, i, None,
                            {5 if norm == 0 else 2: lambda: norm_spread(norm)} if first else {})
                    wait_free(SET_A, f.a + 1, i)
                    project(n + 2, SET_A, i)
                    pe.wait_ge(h_set, nh + 1)
                    project(n + 3, SET_B, i, by_block=True)
                    for j in range(KT):
                        s = j % 2
                        if j % 4 == 0:
                            pe.wait_ge(w_lo, at_step(n + 5 + j // 4, i))
                        if j == 1:
                            pe.wait_ge(h_set, nh + 1 + NB)
                        else:
                            wait_free(s, (f.a, f.b)[s] + 2 + j // 2, i)
                        b = (n + 4 + j // 4) % 2

                        def down(q, blks):
                            m = q * 4 + j % 4
                            return three_passes(lambda blk: ps[:, SETS[s] + blk, 0:TB], wh[b][:, m, :],
                                                wl[b][:, m, :], hh[:, q, :], hl[:, q, :], blks,
                                                q == 0, q == 1)
                        if j == 0:
                            pe.wait_ge(h_lo, nh + 1)
                        last_mm = down(0, range(NB))
                        if j == 0:
                            for blk in range(NB):
                                pe.wait_ge(h_lo, nh + 2 + blk)
                                last_mm = down(1, (blk,))
                        else:
                            last_mm = down(1, range(NB))
                        last_mm.then_inc(full[s], 1)
                return pair

            def x_tile(t):
                pe.wait_ge(x_in[t], 16)
                if t == NTILE:
                    pe.wait_ge(cols_set, 2)
                earlier = [u for u in range(t) if X_BANKS[u] == X_BANKS[t]]
                if earlier:
                    wait_copied(pe, earlier[-1] + 1)
                w = P if t < NTILE else dec
                src = xin[:, t, :] if t < NTILE else xin_s[0:dec, :]
                for j in range(KT):
                    last = pe.transpose(x_ps(t)[:, j, 0:w], src[:, j * P:j * P + P], ident[0:w, 0:w])
                last.then_inc(xt_full, 1)

            def rows_as_columns(n):
                pe.transpose(ps[:, 7, 0:n], rows[0:n, :], ident[0:n, 0:n]).then_inc(rows_t, 1)

            pe.wait_ge(ones_set, 1)
            for _ in range(7):
                pe.matmul(ps[:, 7, 0:P], ones[:], ones[:], start=True, stop=True)
            pe.wait_ge(ones_set, 4)
            x_tile(0)
            pe.wait_ge(gain_in, 16)
            rows_as_columns(KT)
            for t in range(1, TILE_ENDS[1] - 1):
                x_tile(t)
            pe.wait_ge(w_lo, 1)
            pe.wait_ge(w_lo_pool, 1)
            beside = {(0, 3): TILE_ENDS[1] - 1, (1, 1): TILE_ENDS[1], (1, 2): TILE_ENDS[1] + 1, (1, 6): NTILE}
            for blk in range(NB):
                for k in range(KT):
                    pe.wait_ge(xg_lo, KT * blk + k + 1)
                    if (blk, k) in beside:
                        x_tile(beside[blk, k])
                    if (blk, k) == (1, 0):
                        pe.wait_ge(small_in, 16 * (len(ROWS) - 1))
                        pe.wait_ge(cols_set, 1)
                        rows_as_columns(n_rows)
                    last = three_passes(lambda blk: ps[:, blk, 0:TB], wh[0][:, k, :], wl[0][:, k, :],
                                        xh[:, k, :], xl[:, k, :], (blk,), k == 0, k == KT - 1)
            last.then_inc(full[SET_A], 1)
            wait_copied(pe, NTILE + 1)
            pair = ffn(ffn1, 0, 0)
            pair(0, first=True)
            with pe.Fori(1, PAIRS - 1) as i:
                pair(i)
            pair(PAIRS - 1, last=True)

            def project_rank(n, s):
                pe.wait_ge(w_lo, n + 1)
                for k in range(KT):
                    pe.wait_ge(xg_lo, xg_before(1) + k + 1)
                    for x_ in (xh, xl):
                        for blk in range(NB):
                            last = pe.matmul(ps[0:GL_ROWS, SETS[s] + blk, 0:TB], wh[n % 2][:, k, 0:GL_ROWS],
                                             x_[:, k, blk * TB:blk * TB + TB],
                                             start=k == 0 and x_ is xh, stop=k == KT - 1 and x_ is xl)
                    if k == KT - 1:
                        last.then_inc(full[s], 1)
                    if k == 6:
                        norm_sums(1)

            wait_free(*g_gl)
            project_rank(u_gl, SET_A)
            wait_free(*g_va[0])
            project(u_va[0], SET_B, hooks={1: lambda: norm_spread(1)})
            wait_free(*g_va[1])

            def gate_z(c):
                s, use = g_z[c]
                pe.wait_ge(w2_low, 1)
                pe.wait_ge(gl_low, 1)
                wait_free(s, use)
                for blk in range(NB):
                    last = pe.matmul(ps[:, SETS[s] + blk, 0:TB], w2_parts[:, c * P:c * P + P],
                                     gl_parts[:, blk * TB:blk * TB + TB], start=True, stop=True)
                last.then_inc(full[s], 1)

            project(u_va[1], SET_A, hooks={KT - 3: lambda: gate_z(0)})
            pe.wait_ge(ws_masked, 1)
            pe.wait_ge(r_set, 2)
            for h in range(heads):
                last = pe.transpose(ps[:, 6, h * P:h * P + P], ws_in[:, h, :], ident[:])
            last.then_inc(ws_full, 1)
            for i, (u, (s, use)) in enumerate(zip(u_qkv, g_qkv)):
                wait_free(s, use)
                project(u, s, hooks={2: lambda: gate_z(1)} if i == 0 else {})
            pe.wait_ge(ws_set, 1)

            def mixers(p, e, w=P):
                t = 2 * p + e
                first = isinstance(t, int) and t == 0
                sample = w < P
                nblk = 1 if sample else 2
                if first or sample:
                    stat = mix[:, 0:10, t * P:t * P + w]
                else:
                    stat = st_a[:]
                    pe.wait_ge(st_a_set, t)

                def of_pair(bank, c, i0, n):
                    return ps[:, bank, 2 * c * P:2 * c * P + 2 * P].rearrange("p (h i) -> p h i", h=2)[
                        :, :, i0:i0 + n]

                def attention():
                    pe.wait_ge(st_q_set, t + 1)
                    if first:
                        pe.wait_ge(free[SET_B], released[SET_B][g_qkv[6][1]])
                        pe.wait_ge(ke_set, NPAIR)
                    else:
                        pe.wait_ge(a_bounded, t)
                    for c in range(NPAIR):
                        last = pe.matmul(of_pair(5, c, 0, w)[0:w], stat[:, K_ + c, 0:w],
                                         st_q[:, 2 * c:2 * c + 2, 0:w], start=True, stop=True)
                    last.then_inc(a_full, 1)

                if first:
                    attention()
                else:
                    pe.wait_ge(gm_set, t)
                    pe.wait_ge(va_n_set, t)
                for c in range(2):
                    pe.transpose(ps[0:w, 4, c * P:c * P + P], stat[:, KE + c, :], ident[:])
                for c in range(2):
                    pe.transpose(ps[0:w, 4, 2 * P + c * P:3 * P + c * P], stat[:, VA + c, :], ident[:])
                for h in range(heads):
                    if first and h == heads - 1:
                        pe.wait_ge(free[SET_A], released[SET_A][g_qkv[7][1]])
                    last = pe.transpose(ps[0:w, 3, h * P:h * P + P], stat[:, V_ + h, :], ident[:])
                last.then_inc(tile_t, 1)
                if not first:
                    attention()

                n = u_big[0] + e
                b = n % 2
                pe.wait_ge(w_lo, n + 1 + 2 * p)
                pe.wait_ge(free[SET_A], released[SET_A][g_big[0][1]] - 1 + t)

                def beside(ks):
                    for k in ks:
                        last = three_passes(lambda blk: ps[:, blk, 0:TB], wh[b][:, k, :], wl[b][:, k, :],
                                            xh[:, k, :], xl[:, k, :], range(NB), k == 0, k == KT - 1)
                        if k == KT - 1:
                            last.then_inc(full[SET_A], 1)

                beside((0, 1, 2))
                pe.wait_ge(ke_n_set, t + 1)
                pe.wait_ge(v_n_set, t + 1)
                if not first:
                    pe.wait_ge(s0_set, t)
                for m in range(nblk):
                    for h in range(heads):
                        c, q = h // 2, h % 2
                        last = pe.matmul(ps[64 * q:64 * q + 64, 7, (2 * m + c) * P:(2 * m + c + 1) * P],
                                         ke_n[0:w, m, c * P + 64 * q:c * P + 64 * q + 64],
                                         v_n[0:w, h * P:h * P + P], start=True, stop=True)
                last.then_inc(ds_full, 1)
                pe.wait_ge(va_n_set, t + 1)
                for h in range(heads):
                    c, q = h // 2, h % 2
                    last = pe.matmul(ps[64 * q:64 * q + 64, 3, c * P:c * P + w],
                                     va_n[0:w, h * 64:h * 64 + 64], ws_t[0:w, h, 0:w],
                                     start=True, stop=True)
                last.then_inc(gm_full, 1)
                beside((3, 4, 5))
                pe.wait_ge(a_masked, t + 1)
                pe.wait_ge(s1_set, t + (0 if sample else 1))
                if not first:
                    pe.wait_ge(o_set, t)
                for h in range(heads):
                    pe.matmul(ps[:, 6, h * P:h * P + w], v_n[0:w, h * P:h * P + P], a_t[0:w, h, 0:w],
                              start=h == 0, stop=False)
                for c in range(NPAIR):
                    for m in range(nblk):
                        state = s_in if sample else (s0, s1)[m]
                        bw = w // nblk
                        last = pe.matmul(of_pair(6, c, m * bw, bw), state[:, c, :],
                                         st_q[:, 2 * c:2 * c + 2, m * bw:m * bw + bw],
                                         start=False, stop=c == NPAIR - 1 and m == nblk - 1)
                last.then_inc(o_full, 1)
                beside((6, 7))

            over_token_tiles(pe, mixers)

            def o_sums(h):
                if h == 0:
                    pe.wait_ge(o_set, NTILE + 1)
                sums(osq, osq_set, h + 1, os_cols, h * (NTILE + 1))

            def o_spread(h):
                pe.wait_ge(oinv_set, 1)
                if h > 0:
                    pe.wait_ge(o_normed, h)
                spread(h * (NTILE + 1), or_full)

            def o_spread_samples():
                pe.wait_ge(oinv_set, 1)
                for h in range(heads):
                    last = across(or_sample(h), ricol, h * (NTILE + 1) + NTILE)
                last.then_inc(or_samples, 1)

            r_hooks = [{1: lambda: o_sums(0), 2: lambda: o_sums(1), 4: lambda: o_sums(2),
                        5: lambda: o_sums(3)},
                       {0: lambda: (o_spread_samples(), o_spread(0)), 3: lambda: o_spread(1),
                        6: lambda: o_spread(2)},
                       {2: lambda: o_spread(3)}]
            for done_with_bank in (gm_set, va_n_set, a_bounded):
                pe.wait_ge(done_with_bank, NTILE + 1)
            for h in range(1, heads):
                wait_free(*g_r[h])
                project(u_r[h], g_r[h][0], hooks=r_hooks[h - 1], tell_used=h == heads - 1)
            for j in range(KT):
                wait_free(*g_wo[j])
                project(u_wo[j], g_wo[j][0], 0, (y_lo, 0) if j == 0 else None, tell_used=j == KT - 1)

            def p_round(g):
                if g == 0:
                    pe.wait_ge(p_in, 48)
                else:
                    pe.wait_ge(p_copied, g)
                for t in range(4 * g, min(4 * g + 4, NTILE + 1)):
                    w = P if t < NTILE else dec
                    for c in range(2):
                        last = pe.transpose(ps[:, 6 + c, t % 4 * P:t % 4 * P + w],
                                            pnat[0:w, t, c * P:c * P + P], ident[0:w, 0:w])
                last.then_inc(p_full, 1)

            pair = ffn(ffn2, PAIRS, 2, {2 * g + 1: (lambda g=g: p_round(g)) for g in range(NROUND)})
            pair(0, first=True)
            with pe.Fori(1, PAIRS - 1) as i:
                pair(i)
            pair(PAIRS - 1, last=True)

            def ple_proj(j, blks, bank):
                for c in range(2):
                    last = three_passes(lambda blk: ps[:, bank(blk), 0:TB],
                                        wph[:, c, j * P:j * P + P], wpl[:, c, j * P:j * P + P],
                                        hh[:, c, :], hl[:, c, :], blks, c == 0, c == 1)
                return last

            for j in range(KT - 1):
                wait_free(*g_gate[j])
                project(u_ple[j], SET_A, 0, (xg_lo, xg_before(3)) if j == 0 else None,
                        {4: lambda: norm_sums(3), 7: lambda: norm_spread(3)} if j == 0 else {})
                if j == 0:
                    wait_free(*g_proj[0])
                    pe.wait_ge(p_lo, 2)
                    pe.wait_ge(wp_lo, 1)
                else:
                    pe.wait_ge(ple_set, j)
                ple_proj(j, range(NB), lambda blk: SETS[SET_B] + blk).then_inc(full[SET_B], 1)

            def out_tile(t):
                earlier = [u for u in range(t) if fin_bank(u) == fin_bank(t)]
                if earlier:
                    pe.wait_ge(fin_set, earlier[-1] + 1)
                t0 = t * P if t < NTILE else T - P
                for j in range(KT):
                    last = pe.transpose(fin_ps(t)[:, j // 4, j % 4 * P:j % 4 * P + P], x[:, j, t0:t0 + P],
                                        ident[:])
                last.then_inc(fin_full, 1)

            wait_free(*g_gate[KT - 1])
            n = u_ple[KT - 1]
            pe.wait_ge(w_lo, n + 1)
            for blk in range(NB):
                for k in range(KT):
                    if blk == NB - 1 and k == KT // 2:
                        pe.wait_ge(last_added, blk)
                        out_tile(FIN_TILES[1][0])
                    last = three_passes(lambda blk: ps[:, 2 * blk, 0:TB], wh[n % 2][:, k, :], wl[n % 2][:, k, :],
                                        xh[:, k, :], xl[:, k, :], (blk,), k == 0, k == KT - 1)
                last.then_inc(last_gate, 1)
                if blk == 0:
                    pe.wait_ge(ple_set, KT - 1)
                ple_proj(KT - 1, (blk,), lambda blk: 2 * blk + 1).then_inc(last_proj, 1)
                if blk > 0:
                    if blk == 1:
                        pe.wait_ge(x_added, KT - 1)
                    pe.wait_ge(last_added, blk)
                    for t in FIN_TILES[blk - 1][blk - 1:]:
                        out_tile(t)
            pe.wait_ge(last_added, NB)
            for t in FIN_TILES[NB - 1]:
                out_tile(t)

    return nc


_INS = ["x_prompt", "x_sample", "p_prompt", "p_sample", "state_conv", "state_gla", "norm_ffn1",
        "w_ffn1_gate", "w_ffn1_up", "w_ffn1_down", "norm_mix", "w_in", "w_s", "b_s", "conv_w", "w_gate2",
        "b_gate2", "gla_norm", "w_o", "norm_ffn2", "w_ffn2_gate", "w_ffn2_up", "w_ffn2_down", "norm_ple",
        "w_ple_gate", "w_ple_proj", "final_norm"]


def kernel(**inputs):
    import numpy as _np
    import concourse.bacc as _bacc
    from concourse.bass_utils import run_bass_kernel_spmd as _run

    nc = _bacc.Bacc("TRN2", target_bir_lowering=False, num_devices=1)
    arrays, ins = {}, {}
    for name in _INS:
        v = _np.ascontiguousarray(inputs[name])
        arrays[f"in_{name}"] = v
        ins[name] = nc.dram_tensor(f"in_{name}", v.shape, mybir.dt.from_np(v.dtype), kind="ExternalInput").ap()
    depth, _, seq, _ = inputs["p_prompt"].shape
    d = inputs["x_prompt"].shape[2]
    _, batch, dec, _ = inputs["p_sample"].shape
    heads, dk, dv = inputs["state_gla"].shape[2:]
    taps, d_b = inputs["conv_w"].shape[1:]
    d_a = d // 4
    shapes = [(1, seq, d), (batch, dec, d), (depth, 1, taps - 1, d_b), (depth, 1, heads, dk, dv),
              (depth, batch, taps - 1, d_b), (depth, batch, heads, dk, dv), (depth, batch, dec, d_a)]
    outs = [nc.dram_tensor(f"out_{i}", s, F32, kind="ExternalOutput").ap() for i, s in enumerate(shapes)]
    hybrid_trunk(nc, ins, outs)
    got = _run(nc, [arrays], core_ids=[0])
    return tuple(got.results[0][f"out_{i}"] for i in range(len(shapes)))
```
